# Optimizing a Trainium2 kernel written in Bass

```python
import jax, jax.numpy as jnp
from jax import lax
import numpy as np

D_MODEL = 1024
BATCH = 1
SEQ = 4096
DEPTH = 1

CHUNK = 64
LEFT_CHUNKS = 8
BAND_CHUNKS = LEFT_CHUNKS + 1
D_MIX = D_MODEL
D_ATT = D_MIX // 2
D_CONV = D_MIX - D_ATT
N_HEADS = 8
HEAD_DIM = D_ATT // N_HEADS
MAX_REL = 128
N_REL = 2 * MAX_REL + 1
CONV_WIDTH = 31
EPS = 1e-6
SPLITS = (D_ATT, D_ATT, D_ATT, D_ATT, D_CONV, D_CONV, D_CONV)
D_IN = sum(SPLITS)

kernel_name = "hymba_chunk_attn_conformer_conv_layer"

def rmsnorm(x, g):
    xf = x.astype(jnp.float32)
    y = xf * lax.rsqrt(jnp.mean(xf * xf, axis=-1, keepdims=True) + EPS)
    return (y * g.astype(jnp.float32)).astype(x.dtype)

def layernorm(x, g, b):
    xf = x.astype(jnp.float32)
    mu = jnp.mean(xf, axis=-1, keepdims=True)
    var = jnp.mean(jnp.square(xf - mu), axis=-1, keepdims=True)
    y = (xf - mu) * lax.rsqrt(var + EPS)
    return (y * g.astype(jnp.float32) + b.astype(jnp.float32)).astype(x.dtype)

def chunk_attention(q, k, v, rel_bias):
    b, s, _ = q.shape
    nc = s // CHUNK
    band = BAND_CHUNKS * CHUNK
    qc = q.reshape(b, nc, CHUNK, N_HEADS, HEAD_DIM)
    pad = ((0, 0), (LEFT_CHUNKS * CHUNK, 0), (0, 0))
    kp = jnp.pad(k, pad).reshape(b, nc + LEFT_CHUNKS, CHUNK, N_HEADS, HEAD_DIM)
    vp = jnp.pad(v, pad).reshape(b, nc + LEFT_CHUNKS, CHUNK, N_HEADS, HEAD_DIM)
    kb = jnp.concatenate([kp[:, i:i + nc] for i in range(BAND_CHUNKS)], axis=2)
    vb = jnp.concatenate([vp[:, i:i + nc] for i in range(BAND_CHUNKS)], axis=2)
    scale = HEAD_DIM ** -0.5
    scores = jnp.einsum('bnqhd,bnkhd->bhnqk', qc, kb).astype(jnp.float32) * scale
    qi = jnp.arange(CHUNK)[:, None]
    kj = jnp.arange(band)[None, :]
    rel = LEFT_CHUNKS * CHUNK + qi - kj
    idx = jnp.clip(rel, -MAX_REL, MAX_REL) + MAX_REL
    bias = rel_bias.astype(jnp.float32)[:, idx]
    key_chunk = jnp.arange(nc)[:, None] - LEFT_CHUNKS + (jnp.arange(band) // CHUNK)[None, :]
    valid = key_chunk >= 0
    scores = scores + bias[None, :, None, :, :]
    scores = jnp.where(valid[None, None, :, None, :], scores, jnp.float32(-1e30))
    p = jax.nn.softmax(scores, axis=-1).astype(v.dtype)
    out = jnp.einsum('bhnqk,bnkhd->bnqhd', p, vb)
    return out.reshape(b, s, N_HEADS * HEAD_DIM)

def conformer_conv(val, gate_glu, dw_w, dw_b, ln_g, ln_b, w_pw, b_pw):
    hg = val * jax.nn.sigmoid(gate_glu)
    kern = dw_w.reshape(CONV_WIDTH, 1, D_CONV).astype(hg.dtype)
    hc = lax.conv_general_dilated(
        hg, kern, window_strides=(1,), padding=[(CONV_WIDTH - 1, 0)],
        dimension_numbers=('NWC', 'WIO', 'NWC'), feature_group_count=D_CONV)
    hc = hc + dw_b
    hn = layernorm(hc, ln_g, ln_b)
    hs = jax.nn.silu(hn)
    return hs @ w_pw + b_pw

def setup_inputs(seed: int = 0) -> dict:
    key = jax.random.key(seed)
    ks = jax.random.split(key, 12)
    f = jnp.float32
    x = jax.random.normal(ks[0], (BATCH, SEQ, D_MODEL), f)
    pre_norm_g = 1.0 + 0.05 * jax.random.normal(ks[1], (DEPTH, D_MODEL), f)
    w_in = jax.random.normal(ks[2], (DEPTH, D_MODEL, D_IN), f) * D_MODEL ** -0.5
    rel_bias = 0.2 * jax.random.normal(ks[3], (DEPTH, N_HEADS, N_REL), f)
    dw_w = jax.random.normal(ks[4], (DEPTH, CONV_WIDTH, D_CONV), f) * CONV_WIDTH ** -0.5
    dw_b = 0.02 * jax.random.normal(ks[5], (DEPTH, D_CONV), f)
    conv_ln_g = 1.0 + 0.05 * jax.random.normal(ks[6], (DEPTH, D_CONV), f)
    conv_ln_b = 0.02 * jax.random.normal(ks[7], (DEPTH, D_CONV), f)
    w_pw = jax.random.normal(ks[8], (DEPTH, D_CONV, D_CONV), f) * D_CONV ** -0.5
    b_pw = 0.02 * jax.random.normal(ks[9], (DEPTH, D_CONV), f)
    w_out = jax.random.normal(ks[10], (DEPTH, D_MIX, D_MODEL), f) * D_MIX ** -0.5
    post_norm_g = 1.0 + 0.05 * jax.random.normal(ks[11], (DEPTH, D_MODEL), f)
    return {"x": x, "pre_norm_g": pre_norm_g, "w_in": w_in, "rel_bias": rel_bias,
            "dw_w": dw_w, "dw_b": dw_b, "conv_ln_g": conv_ln_g, "conv_ln_b": conv_ln_b,
            "w_pw": w_pw, "b_pw": b_pw, "w_out": w_out, "post_norm_g": post_norm_g}

def reference(x, pre_norm_g, w_in, rel_bias, dw_w, dw_b, conv_ln_g, conv_ln_b,
              w_pw, b_pw, w_out, post_norm_g):
    split_pts = list(np.cumsum(SPLITS)[:-1])
    for l in range(DEPTH):
        h = rmsnorm(x, pre_norm_g[l])
        u = h @ w_in[l]
        q, k, v, g_att, c_val, c_glu, g_conv = jnp.split(u, split_pts, axis=-1)
        a = chunk_attention(q, k, v, rel_bias[l]) * jax.nn.silu(g_att)
        c = conformer_conv(c_val, c_glu, dw_w[l], dw_b[l], conv_ln_g[l], conv_ln_b[l],
                           w_pw[l], b_pw[l]) * jax.nn.silu(g_conv)
        y = jnp.concatenate([a, c], axis=-1) @ w_out[l]
        x = x + rmsnorm(y, post_norm_g[l])
    return x


_drawn_inputs = setup_inputs


def setup_inputs(seed=0):
    import zlib

    import numpy as np

    out = dict(_drawn_inputs(seed))
    spreads = {}
    factors = {'rel_bias': 4.202, 'conv_ln_b': 4.067}
    for name, (base, spread) in spreads.items():
        noise = np.random.default_rng([zlib.crc32(name.encode()), seed]).standard_normal(out[name].shape)
        drawn = base * np.exp(spread * noise) if base else spread * noise
        out[name] = __import__('jax').numpy.asarray(drawn.astype(out[name].dtype))
    for name, factor in factors.items():
        out[name] = (out[name] * factor).astype(out[name].dtype)
    return out
```

```python
from contextlib import ExitStack

import concourse.bass as bass
from concourse import mybir

F32 = mybir.dt.float32
F32R = mybir.dt.float32r
BF16 = mybir.dt.bfloat16
ALU = mybir.AluOpType
ACT = mybir.ActivationFunctionType

P = 128
D_MODEL = 1024
SEQ = 4096
D_HALF = 512
HEADS = 8
HEAD_DIM = D_HALF // HEADS
CHUNK = 64
LEFT = 8 * CHUNK
MAX_REL = 128
TAPS = 31
HALO = TAPS - 1
PAD = 32
EPS = 1e-6
MASKED = -1e30

KT = D_MODEL // P
CT = D_HALF // P
SUB = 256
BLK = 512
NBLK = SEQ // BLK
DMA = 16
TAPS_1 = 14
TAPS_2 = TAPS - TAPS_1

COL_Q, COL_K, COL_V, COL_GA, COL_VAL, COL_GLU, COL_GC = (n * D_HALF for n in range(7))


def is_first(i):
    return isinstance(i, int) and i == 0


def f32(ap):
    return ap.bitcast(F32)


class Tools:

    def __init__(self, nc, ctx, tag):
        self.nc, self.ctx, self.tag = nc, ctx, tag

    def sb(self, name, shape, dt=F32):
        return self.ctx.enter_context(self.nc.sbuf_tensor(f"{self.tag}_{name}", shape, dt))

    def bank(self, name, cols=512):
        return self.ctx.enter_context(self.nc.psum_tensor(f"{self.tag}_{name}", [P, cols], F32))

    def sem(self, name):
        return self.ctx.enter_context(self.nc.semaphore(f"{self.tag}_{name}"))

    def sems(self, name, n):
        return [self.sem(f"{name}{j}") for j in range(n)]


def setup(nc, io, K, D):
    with ExitStack() as ctx:
        T = Tools(nc, ctx, "s")
        dw = T.sb("dw", [TAPS, D_HALF])
        ps = T.bank("ps")
        zero = T.sb("zero", [P, CT, HALO])
        rel = T.sb("rel", [HEADS, 2 * MAX_REL + 1])
        rev = T.sb("rev", [HEADS, 3 * P - 1])
        rel_in, rev_ok, rev_out = T.sem("rel_in"), T.sem("rev_ok"), T.sem("rev_out")
        zeroed, ident_ok, loaded = T.sem("zeroed"), T.sem("ident_ok"), T.sem("loaded")
        zero_ok, zero_out = T.sem("zero_ok"), T.sem("zero_out")
        dwt_ps, done, pdone = T.sem("dwt_ps"), T.sem("done"), T.sem("pdone")
        block = ctx.enter_context(nc.Block())

        @block.sync
        def _(sp):
            sp.dma_start(dw[:, :], io["dw_w"][0]).then_inc(loaded, DMA)
            sp.dma_start(rel[:, :], io["rel_bias"][0]).then_inc(rel_in, DMA)
            for dst, src in ((K["g_pre"], "pre_norm_g"), (K["dw_b"], "dw_b"), (K["ln_g"], "conv_ln_g"),
                             (K["ln_b"], "conv_ln_b"), (K["b_pw"], "b_pw")):
                sp.dma_start(dst[:, :], io[src][0].rearrange("(t p) -> p t", p=P),
                             allow_slow_non_contiguous=True).then_inc(loaded, DMA)
            sp.wait_ge(loaded, 6 * DMA)
            sp.wait_ge(zero_ok, 1)
            sp.dma_start(D["hg"].rearrange("(c p) t -> p c t", p=P)[:, :, PAD - HALO:PAD], zero[:, :, :]).then_inc(zero_out, DMA)
            sp.wait_ge(zero_out, DMA)
            sp.wait_ge(rev_ok, 2)
            sp.dma_start(D["rev"], rev[:, None, :].broadcast_to([HEADS, P, 3 * P - 1])).then_inc(rev_out, DMA)
            sp.wait_ge(rev_out, DMA)

        @block.gpsimd
        def _(pool):
            nc.gpsimd.memset(K["ident"][:, :], 0.0).then_inc(zeroed, 1)
            nc.gpsimd.memset(K["eps"][:, :], EPS).then_inc(pdone, 1)
            nc.gpsimd.memset(K["mhalf"][:, :], -0.5).then_inc(pdone, 1)
            nc.gpsimd.memset(K["ones"][:, :], 1.0 / D_HALF).then_inc(pdone, 1)
            pool.wait_ge(zeroed, 1)
            nc.gpsimd.affine_select(out=K["ident"][:, :], in_=K["ident"][:, :], compare_op=ALU.not_equal,
                                    fill=1.0, base=0, pattern=[[-1, P]], channel_multiplier=1).then_inc(ident_ok, 1)
            pool.wait_ge(pdone, 3)

        @block.tensor
        def _(pe):
            pe.wait_ge(ident_ok, 1)
            pe.wait_ge(loaded, 6 * DMA)
            for c in range(CT):
                mm = nc.tensor.transpose(ps[:, c * TAPS:(c + 1) * TAPS], dw[:, c * P:(c + 1) * P],
                                         K["ident"][0:TAPS, 0:TAPS])
            mm.then_inc(dwt_ps, 1)

        @block.vector
        def _(dve):
            nc.vector.memset(zero[:, :, :], 0.0).then_inc(zero_ok, 1)
            dve.wait_ge(rel_in, DMA)
            nc.vector.tensor_copy(rev[:, 0:P - 1], rel[:, 2 * MAX_REL:].broadcast_to([HEADS, P - 1])).then_inc(rev_ok, 1)
            nc.vector.tensor_copy(rev[:, P - 1:], rel[:, 2 * MAX_REL:0:-1]).then_inc(rev_ok, 1)
            dve.wait_ge(loaded, 6 * DMA)
            nc.vector.tensor_scalar(K["ln_gh"][:, :], K["ln_g"][:, :], 0.5, None, ALU.mult).then_inc(done, 1)
            nc.vector.tensor_scalar(K["ln_bh"][:, :], K["ln_b"][:, :], 0.5, None, ALU.mult).then_inc(done, 1)
            nc.vector.tensor_scalar(K["b_pw2"][:, :], K["b_pw"][:, :], 2.0, None, ALU.mult).then_inc(done, 1)
            dve.wait_ge(dwt_ps, 1)
            nc.vector.tensor_scalar(K["dwt"][:, :], ps[:, 0:CT * TAPS], 0.5, None, ALU.mult).then_inc(done, 1)
            dve.wait_ge(done, 4)


class Hidden:

    def __init__(self, nc, T, K, x):
        self.nc, self.K, self.x = nc, K, x
        self.xb = [T.sb(f"x{s}", [P, 2, D_MODEL]) for s in range(2)]
        self.hi = [T.sb(f"hT_hi{s}", [P, KT, SUB], F32R) for s in range(2)]
        self.lo = [T.sb(f"hT_lo{s}", [P, KT, SUB], F32R) for s in range(2)]
        self.junk = T.sb("junk", [P, D_MODEL], BF16)
        self.ms = T.sb("ms", [P, 4])
        self.mse = T.sb("mse", [P, 4])
        self.rstd = T.sb("rstd", [P, 4])
        self.tb = [T.bank(f"tb{j}") for j in range(2)]
        self.x_in = T.sems("x_in", 2)
        self.squared, self.eps_added, self.rstd_ok = T.sem("squared"), T.sem("eps_added"), T.sem("rstd_ok")
        self.h_ok, self.t_ps, self.t_hi, self.t_lo = (T.sem(n) for n in ("h_ok", "t_ps", "t_hi", "t_lo"))

    def load(self, sp, i, s):
        rows = self.x[bass.ds((2 * i + s) * SUB, SUB), :]
        sp.dma_start(self.xb[s][:, :, :], rows.rearrange("(t p) d -> p t d", p=P)).then_inc(self.x_in[s], DMA)

    def square(self, act, i, s):
        act.wait_ge(self.x_in[s], DMA * (i + 1))
        for t in range(2):
            if t == 1:
                act.wait_ge(self.squared, 2 * (2 * i + s) + 1)
            self.nc.scalar.activation(self.junk[:, :], self.xb[s][:, t, :], ACT.Square, scale=D_MODEL ** -0.5,
                                      accum_out=self.ms[:, 2 * s + t:2 * s + t + 1]).then_inc(self.squared, 1)

    def power(self, pool, i, s):
        b = 2 * i + s
        w = slice(2 * s, 2 * s + 2)
        pool.wait_ge(self.squared, 2 * (b + 1))
        self.nc.gpsimd.tensor_tensor(self.mse[:, w], self.ms[:, w], self.K["eps"][:, 0:2], ALU.add).then_inc(self.eps_added, 1)
        pool.wait_ge(self.eps_added, b + 1)
        self.nc.gpsimd.tensor_tensor(self.rstd[:, w], self.mse[:, w], self.K["mhalf"][:, 0:2], ALU.pow).then_inc(self.rstd_ok, 1)

    def scale(self, dve, i, s):
        dve.wait_ge(self.rstd_ok, 2 * i + s + 1)
        for t in range(2):
            self.nc.vector.tensor_scalar(self.xb[s][:, t, :], self.xb[s][:, t, :],
                                         self.rstd[:, 2 * s + t:2 * s + t + 1], None, ALU.mult).then_inc(self.h_ok, 1)

    def turn(self, pe, i, s, n, first=False):
        b = 2 * i + s
        if n == 0:
            pe.wait_ge(self.h_ok, 2 * (b + 1))
        if not first or n >= 2:
            pe.wait_ge(self.t_lo, 4 * b + n - 1)
        for k in range(2):
            for t in range(2):
                mm = self.nc.tensor.transpose(self.tb[n % 2][:, k * SUB + t * P:k * SUB + (t + 1) * P],
                                              self.xb[s][:, t, (2 * n + k) * P:(2 * n + k + 1) * P],
                                              self.K["ident"][:, :])
        mm.then_inc(self.t_ps, 1)

    def split_hi(self, act, i, s, n):
        act.wait_ge(self.t_ps, 4 * (2 * i + s) + n + 1)
        self.nc.scalar.activation(self.hi[s][:, 2 * n:2 * n + 2, :], self.tb[n % 2][:, :].rearrange("p (k t) -> p k t", k=2),
                                  ACT.Copy).then_inc(self.t_hi, 1)

    def split_lo(self, dve, i, s, n):
        dve.wait_ge(self.t_hi, 4 * (2 * i + s) + n + 1)
        self.nc.vector.tensor_tensor(self.lo[s][:, 2 * n:2 * n + 2, :],
                                     self.tb[n % 2][:, :].rearrange("p (k t) -> p k t", k=2),
                                     f32(self.hi[s][:, 2 * n:2 * n + 2, :]), ALU.subtract).then_inc(self.t_lo, 1)


class Weights:

    def __init__(self, nc, T, raw):
        self.nc, self.raw, self.jobs = nc, raw, []
        self.raw_in = T.sems("raw_in", len(raw))
        self.w_hi, self.w_lo = T.sem("w_hi"), T.sem("w_lo")

    def add(self, src, hi, lo, gain=None):
        self.jobs.append((src, hi, lo, gain))
        return len(self.jobs)

    def load(self, sp):
        n_raw = len(self.raw)
        for n, (src, hi, _, _) in enumerate(self.jobs):
            if n >= n_raw:
                sp.wait_ge(self.w_lo, n - n_raw + 1)
            sp.dma_start(self.raw[n % n_raw][:, 0:src.shape[1]], src).then_inc(self.raw_in[n % n_raw], DMA)

    def split_hi(self, act, n0=0, n1=None):
        for n, (src, hi, _, gain) in list(enumerate(self.jobs))[n0:n1]:
            r = self.raw[n % len(self.raw)][:, 0:src.shape[1]]
            act.wait_ge(self.raw_in[n % len(self.raw)], DMA * (n // len(self.raw) + 1))
            if gain is None:
                self.nc.scalar.activation(hi, r, ACT.Copy).then_inc(self.w_hi, 1)
            else:
                self.nc.scalar.activation(hi, r, ACT.Copy, scale=gain).then_inc(self.w_hi, 1)

    def split_lo(self, dve, n0=0, n1=None):
        for n, (src, hi, lo, gain) in list(enumerate(self.jobs))[n0:n1]:
            r = self.raw[n % len(self.raw)][:, 0:src.shape[1]]
            dve.wait_ge(self.w_hi, n + 1)
            if gain is None:
                self.nc.vector.tensor_tensor(lo, r, f32(hi), ALU.subtract).then_inc(self.w_lo, 1)
            else:
                self.nc.vector.scalar_tensor_tensor(lo, r, gain, f32(hi), ALU.mult, ALU.subtract).then_inc(self.w_lo, 1)


def product(nc, out, stat_hi, stat_lo, mov_hi, mov_lo, tiles, before=None):
    for k in range(tiles):
        if before:
            before(k)
        nc.tensor.matmul(out, stat_hi(k), mov_hi(k), start=(k == 0), stop=False)
        nc.tensor.matmul(out, stat_hi(k), mov_lo(k), start=False, stop=False)
        mm = nc.tensor.matmul(out, stat_lo(k), mov_hi(k), start=False, stop=(k == tiles - 1))
    return mm


def pass_1(nc, io, K, D):
    w_in = io["w_in"][0]
    with ExitStack() as ctx:
        T = Tools(nc, ctx, "p1")
        H = Hidden(nc, T, K, io["x"][0])
        GRP = 2 * D_HALF
        w_hi = [T.sb(f"w_hi{j}", [P, KT, GRP], F32R) for j in range(2)]
        w_lo = [T.sb(f"w_lo{j}", [P, KT, GRP], F32R) for j in range(2)]
        glu_t = T.sb("glu_t", [P, 2, SUB])
        hg = [T.sb(f"hg{s}", [P, CT, HALO + SUB]) for s in range(2)]
        acc = T.sb("acc", [P, CT, SUB])
        st = [T.sb(f"st{j}", [P, 2, 2, SUB], F32R) for j in range(2)]
        W = Weights(nc, T, [H.xb[1][:, 0, :], H.xb[1][:, 1, :], acc[:, :, :].rearrange("p c t -> p (c t)"),
                            *(f32(s[:, :, :, :]).rearrange("p a c t -> p (a c t)") for s in st)])
        for j, col in enumerate((COL_VAL, COL_Q)):
            for k in range(KT):
                W.add(w_in[k * P:(k + 1) * P, col:col + GRP], w_hi[j][:, k, :], w_lo[j][:, k, :], K["g_pre"][:, k:k + 1])
        banks = [T.bank(f"pb{j}") for j in range(4)]
        free = T.sems("free", 4)
        p_ps = T.sem("p_ps")
        tanh_ok, hg_ok, halo_ok, tapped, hg_zero = (T.sem(n) for n in ("tanh_ok", "hg_ok", "halo_ok", "tapped", "hg_zero"))
        qk_hi, qk_lo = T.sem("qk_hi"), T.sem("qk_lo")
        hg_out, acc_out, st_out = T.sems("hg_out", 2), T.sems("acc_out", 2), T.sems("st_out", 2)
        block = ctx.enter_context(nc.Block())

        UNITS = [(0, D_HALF), (0, 0), (0, D_HALF + 2 * P), (0, 2 * P),
                 (1, 0), (1, 2 * P), (1, D_HALF), (1, D_HALF + 2 * P)]
        NU = len(UNITS)
        NTAP = CT * TAPS_1

        @block.sync
        def _(sp):
            H.load(sp, 0, 0)
            W.load(sp)
            sp.wait_ge(W.w_lo, len(W.jobs))
            H.load(sp, 0, 1)

            def body(i, last):
                for s in range(2):
                    b = 2 * i + s
                    cols = bass.ds(b * SUB + PAD, SUB)
                    if not last:
                        sp.wait_ge(H.t_ps, 4 * (b + 1))
                        H.load(sp, i + 1, s)
                    for pair in range(2):
                        sp.wait_ge(hg_ok, 2 * b + pair + 1)
                        sp.dma_start(D["hg"].rearrange("(c p) t -> p c t", p=P)[:, 2 * pair:2 * pair + 2, cols],
                                     hg[s][:, 2 * pair:2 * pair + 2, HALO:]).then_inc(hg_out[s], DMA)
                    for u in range(4):
                        if u == 2:
                            acc_store(b, cols, 0)
                        sp.wait_ge(qk_lo, 4 * b + u + 1)
                        dst = D["q" if u < 2 else "k"].rearrange("a (c p) t -> p a c t", p=P)
                        for part in range(2):
                            sp.dma_start(dst[:, part, 2 * (u % 2):2 * (u % 2) + 2, cols],
                                         f32(st[u % 2][:, part, :, :])).then_inc(st_out[u % 2], DMA)
                    acc_store(b, cols, 1)

            def acc_store(b, cols, pair):
                sp.wait_ge(tapped, NTAP * b + (pair + 1) * NTAP // 2)
                sp.dma_start(D["acc"].rearrange("(c p) t -> p c t", p=P)[:, 2 * pair:2 * pair + 2, cols],
                             acc[:, 2 * pair:2 * pair + 2, :]).then_inc(acc_out[pair], DMA)

            with sp.Fori(0, NBLK - 1) as i:
                body(i, False)
            body(NBLK - 1, True)
            for s in range(2):
                sp.wait_ge(hg_out[s], 2 * NBLK * DMA)
                sp.wait_ge(acc_out[s], 2 * NBLK * DMA)
                sp.wait_ge(st_out[s], 8 * NBLK * DMA)

        @block.gpsimd
        def _(pool):
            H.power(pool, 0, 0)

            def body(i, last):
                H.power(pool, i, 1)
                if not last:
                    H.power(pool, i + 1, 0)

            with pool.Fori(0, NBLK - 1) as i:
                body(i, False)
            body(NBLK - 1, True)

        @block.scalar
        def _(act):
            H.square(act, 0, 0)
            for n in range(4):
                H.split_hi(act, 0, 0, n)
            W.split_hi(act)

            def body(i, last):
                for s in range(2):
                    b = 2 * i + s
                    nxt = None if last and s == 1 else (i + s, 1 - s)
                    if nxt:
                        H.square(act, *nxt)
                    for u in range(NU):
                        m = NU * b + u
                        if u in (0, 2):
                            act.wait_ge(p_ps, m + 1)
                            if u > 0 or not is_first(b):
                                act.wait_ge(hg_ok, 2 * b + u // 2)
                            nc.scalar.activation(glu_t[:, :, :], banks[u % 4][:, :].rearrange("p (c t) -> p c t", c=2),
                                                 ACT.Tanh, scale=0.5).then_inc(tanh_ok, 1)
                        if u >= 4:
                            j = u - 4
                            act.wait_ge(p_ps, m + 1)
                            if j >= 2 or not is_first(b):
                                act.wait_ge(st_out[j % 2], 2 * DMA * (2 * b + j // 2))
                            nc.scalar.activation(st[j % 2][:, 0, :, :], banks[u % 4][:, :].rearrange("p (c t) -> p c t", c=2),
                                                 ACT.Copy, scale=HEAD_DIM ** -0.5 if j < 2 else 1.0).then_inc(qk_hi, 1)
                        if u % 2 == 1 and nxt:
                            H.split_hi(act, *nxt, u // 2)

            body(0, False)
            with act.Fori(1, NBLK - 1) as i:
                body(i, False)
            body(NBLK - 1, True)

        @block.vector
        def _(dve):
            nc.vector.memset(hg[1][:, :, SUB:], 0.0).then_inc(hg_zero, 1)
            H.scale(dve, 0, 0)
            for n in range(4):
                H.split_lo(dve, 0, 0, n)
            W.split_lo(dve)
            dve.wait_ge(hg_zero, 1)

            def taps(b, s, n0, n1):
                for n in range(n0, n1):
                    pair, rest = divmod(n, 2 * TAPS_1)
                    tap, c = rest // 2, 2 * pair + rest % 2
                    if tap == 0:
                        if rest == 0:
                            dve.wait_ge(hg_ok, 2 * b + pair + 1)
                            dve.wait_ge(halo_ok, 2 * b + pair + 1)
                            if not is_first(b):
                                dve.wait_ge(acc_out[pair], DMA * b)
                        nc.vector.tensor_scalar(acc[:, c, :], hg[s][:, c, 0:SUB], K["dwt"][:, c * TAPS:c * TAPS + 1],
                                                K["dw_b"][:, c:c + 1], ALU.mult, ALU.add).then_inc(tapped, 1)
                    else:
                        dve.wait_ge(tapped, NTAP * b + n - 1)
                        nc.vector.scalar_tensor_tensor(acc[:, c, :], hg[s][:, c, tap:tap + SUB],
                                                       K["dwt"][:, c * TAPS + tap:c * TAPS + tap + 1], acc[:, c, :],
                                                       ALU.mult, ALU.add).then_inc(tapped, 1)

            def body(i, last):
                for s in range(2):
                    b = 2 * i + s
                    nxt = None if last and s == 1 else (i + s, 1 - s)
                    if nxt:
                        H.scale(dve, *nxt)
                    for pair in range(2):
                        w = slice(2 * pair, 2 * pair + 2)
                        if pair == 0 and not is_first(i):
                            dve.wait_ge(hg_out[s], 2 * DMA * i)
                        if pair == 0 and not is_first(b):
                            dve.wait_ge(tapped, NTAP * b)
                        nc.vector.tensor_copy(hg[s][:, w, 0:HALO], hg[1 - s][:, w, SUB:]).then_inc(halo_ok, 1)
                        dve.wait_ge(tanh_ok, 2 * b + pair + 1)
                        dve.wait_ge(p_ps, NU * b + 2 * pair + 2)
                        nc.vector.scalar_tensor_tensor(hg[s][:, w, HALO:], glu_t[:, :, :], 1.0,
                                                       banks[2 * pair + 1][:, :].rearrange("p (c t) -> p c t", c=2),
                                                       ALU.add, ALU.mult).then_inc(hg_ok, 1)
                        if nxt:
                            H.split_lo(dve, *nxt, pair)
                        taps(b, s, pair * NTAP // 4, (pair + 1) * NTAP // 4)
                    for j in range(4):
                        u = 4 + j
                        dve.wait_ge(qk_hi, 4 * b + j + 1)
                        nc.vector.scalar_tensor_tensor(st[j % 2][:, 1, :, :], banks[u % 4][:, :].rearrange("p (c t) -> p c t", c=2),
                                                       HEAD_DIM ** -0.5 if j < 2 else 1.0, f32(st[j % 2][:, 0, :, :]),
                                                       ALU.mult, ALU.subtract).then_inc(qk_lo, 1)
                        if j % 2 == 1 and nxt:
                            H.split_lo(dve, *nxt, 2 + j // 2)
                        taps(b, s, NTAP // 2 + j * NTAP // 8, NTAP // 2 + (j + 1) * NTAP // 8)

            body(0, False)
            with dve.Fori(1, NBLK - 1) as i:
                body(i, False)
            body(NBLK - 1, True)

        @block.tensor
        def _(pe):
            for n in range(4):
                H.turn(pe, 0, 0, n, first=True)

            def body(i, last):
                for s in range(2):
                    b = 2 * i + s
                    nxt = None if last and s == 1 else (i + s, 1 - s)
                    pe.wait_ge(H.t_lo, 4 * (b + 1))
                    for u, (j, col) in enumerate(UNITS):
                        if u == 0:
                            pe.wait_ge(W.w_lo, KT)
                        if u == 4:
                            pe.wait_ge(W.w_lo, 2 * KT)
                        if u >= 4:
                            if u % 2 == 0:
                                pe.wait_ge(tanh_ok, 2 * b + (u - 4) // 2 + 1)
                            else:
                                pe.wait_ge(hg_ok, 2 * b + (u - 5) // 2 + 1)
                        else:
                            pe.wait_ge(qk_lo, 4 * b - 4 + u + 1) if not is_first(b) else None
                        for c in range(2):
                            mm = product(nc, banks[u % 4][:, c * SUB:(c + 1) * SUB],
                                         lambda k: w_hi[j][:, k, col + c * P:col + (c + 1) * P],
                                         lambda k: w_lo[j][:, k, col + c * P:col + (c + 1) * P],
                                         lambda k: H.hi[s][:, k, :], lambda k: H.lo[s][:, k, :], KT)
                        mm.then_inc(p_ps, 1)
                        if u % 2 == 1 and nxt:
                            H.turn(pe, *nxt, u // 2)

            body(0, False)
            with pe.Fori(1, NBLK - 1) as i:
                body(i, False)
            body(NBLK - 1, True)


def pass_2(nc, io, K, D):
    w_in = io["w_in"][0]
    with ExitStack() as ctx:
        T = Tools(nc, ctx, "p2")
        H = Hidden(nc, T, K, io["x"][0])
        GRP = 3 * D_HALF
        w_hi, w_lo = T.sb("w_hi", [P, KT, GRP], F32R), T.sb("w_lo", [P, KT, GRP], F32R)
        vst = T.sb("vst", [P, 2, HEADS, 2, HEAD_DIM], F32R)
        tanh = T.sb("tanh", [P, 2, 2, SUB])
        gate = T.sb("gate", [P, 2, 2, SUB])
        hgl = T.sb("hgl", [P, CT, HALO + BLK])
        acc = T.sb("acc", [P, CT, BLK])
        W = Weights(nc, T, [H.xb[1][:, 0, :], H.xb[1][:, 1, :],
                            *(f32(vst[:, t, :, :, :]).rearrange("p h a d -> p (h a d)") for t in range(2)),
                            *(g[:, :, :, :].rearrange("p a c t -> p (a c t)") for g in (tanh, gate))])
        for k in range(KT):
            W.add(w_in[k * P:(k + 1) * P, COL_V:COL_V + 2 * D_HALF], w_hi[:, k, 0:2 * D_HALF], w_lo[:, k, 0:2 * D_HALF], K["g_pre"][:, k:k + 1])
        for k in range(KT):
            W.add(w_in[k * P:(k + 1) * P, COL_GC:COL_GC + D_HALF], w_hi[:, k, 2 * D_HALF:], w_lo[:, k, 2 * D_HALF:], K["g_pre"][:, k:k + 1])
        banks = [T.bank(f"pb{j}") for j in range(6)]
        p_ps = T.sem("p_ps")
        v_hi, v_lo, tanh_ok, gate_ok, tapped = (T.sem(n) for n in ("v_hi", "v_lo", "tanh_ok", "gate_ok", "tapped"))
        v_out, gate_out = T.sem("v_out"), T.sems("gate_out", 2)
        hg_in, acc_in, acc_out = T.sems("hg_in", 2), T.sems("acc_in", 2), T.sems("acc_out", 2)
        block = ctx.enter_context(nc.Block())

        NTAP = CT * TAPS_2
        UNITS = 6

        @block.sync
        def _(sp):
            H.load(sp, 0, 0)
            W.load(sp)
            sp.wait_ge(W.w_lo, len(W.jobs))
            H.load(sp, 0, 1)

            def conv_load(i, pair):
                w = slice(2 * pair, 2 * pair + 2)
                sp.dma_start(hgl[:, w, :], D["hg"].rearrange("(c p) t -> p c t", p=P)[:, w, bass.ds(i * BLK + PAD - HALO, HALO + BLK)]).then_inc(hg_in[pair], DMA)
                sp.dma_start(acc[:, w, :], D["acc"].rearrange("(c p) t -> p c t", p=P)[:, w, bass.ds(i * BLK + PAD, BLK)]).then_inc(acc_in[pair], DMA)

            for pair in range(2):
                conv_load(0, pair)

            def body(i, last):
                for s in range(2):
                    b = 2 * i + s
                    if not last:
                        sp.wait_ge(H.t_ps, 4 * (b + 1))
                        H.load(sp, i + 1, s)
                    sp.wait_ge(v_lo, 2 * (b + 1))
                    sp.dma_start(D["v"][bass.ds(b * SUB, SUB), :].rearrange("(t p) c -> p t c", p=P),
                                 f32(vst[:, :, :, :, :]).rearrange("p t h a d -> p t (h a d)")).then_inc(v_out, DMA)
                    for u in range(4):
                        sp.wait_ge(gate_ok, 4 * b + u + 1)
                        sp.dma_start(D["ga" if u < 2 else "gc"].rearrange("(c p) t -> p c t", p=P)[:, 2 * (u % 2):2 * (u % 2) + 2, bass.ds(b * SUB + PAD, SUB)],
                                     gate[:, u % 2, :, :]).then_inc(gate_out[u % 2], DMA)
                    w = slice(2 * s, 2 * s + 2)
                    sp.wait_ge(tapped, NTAP * i + (s + 1) * NTAP // 2)
                    sp.dma_start(D["acc2"].rearrange("(c p) t -> p c t", p=P)[:, w, bass.ds(i * BLK + PAD, BLK)], acc[:, w, :]).then_inc(acc_out[s], DMA)
                    if not last:
                        sp.wait_ge(acc_out[s], DMA * (i + 1))
                        conv_load(i + 1, s)

            with sp.Fori(0, NBLK - 1) as i:
                body(i, False)
            body(NBLK - 1, True)
            sp.wait_ge(v_out, 2 * NBLK * DMA)
            for s in range(2):
                sp.wait_ge(gate_out[s], 4 * NBLK * DMA)
                sp.wait_ge(acc_out[s], NBLK * DMA)

        @block.gpsimd
        def _(pool):
            H.power(pool, 0, 0)

            def body(i, last):
                H.power(pool, i, 1)
                if not last:
                    H.power(pool, i + 1, 0)

            with pool.Fori(0, NBLK - 1) as i:
                body(i, False)
            body(NBLK - 1, True)

        @block.scalar
        def _(act):
            H.square(act, 0, 0)
            for n in range(4):
                H.split_hi(act, 0, 0, n)
            W.split_hi(act)

            def body(i, last):
                for s in range(2):
                    b = 2 * i + s
                    nxt = None if last and s == 1 else (i + s, 1 - s)
                    if nxt:
                        H.square(act, *nxt)
                    for u in range(UNITS):
                        act.wait_ge(p_ps, UNITS * b + u + 1)
                        if u < 2:
                            if u == 0 and not is_first(b):
                                act.wait_ge(v_out, DMA * b)
                            nc.scalar.activation(vst[:, u, :, 0, :], banks[u][:, :].rearrange("p (h d) -> p h d", h=HEADS),
                                                 ACT.Copy).then_inc(v_hi, 1)
                        else:
                            j = u - 2
                            if j >= 2 or not is_first(b):
                                act.wait_ge(gate_ok, 4 * b + j - 1)
                            nc.scalar.activation(tanh[:, j % 2, :, :], banks[u][:, :].rearrange("p (c t) -> p c t", c=2),
                                                 ACT.Tanh, scale=0.5).then_inc(tanh_ok, 1)
                        if u in (0, 2, 4, 5) and nxt:
                            H.split_hi(act, *nxt, (0, 2, 4, 5).index(u))

            body(0, False)
            with act.Fori(1, NBLK - 1) as i:
                body(i, False)
            body(NBLK - 1, True)

        @block.vector
        def _(dve):
            H.scale(dve, 0, 0)
            for n in range(4):
                H.split_lo(dve, 0, 0, n)
            W.split_lo(dve)

            def taps(i, n0, n1):
                for n in range(n0, n1):
                    pair, rest = divmod(n, 2 * TAPS_2)
                    tap, c = TAPS_1 + rest // 2, 2 * pair + rest % 2
                    if rest == 0:
                        dve.wait_ge(hg_in[pair], DMA * (i + 1))
                        dve.wait_ge(acc_in[pair], DMA * (i + 1))
                    elif rest >= 2:
                        dve.wait_ge(tapped, NTAP * i + n - 1)
                    nc.vector.scalar_tensor_tensor(acc[:, c, :], hgl[:, c, tap:tap + BLK],
                                                   K["dwt"][:, c * TAPS + tap:c * TAPS + tap + 1], acc[:, c, :],
                                                   ALU.mult, ALU.add).then_inc(tapped, 1)

            def body(i, last):
                for s in range(2):
                    b = 2 * i + s
                    nxt = None if last and s == 1 else (i + s, 1 - s)
                    if nxt:
                        H.scale(dve, *nxt)
                    for u in range(UNITS):
                        if u < 2:
                            dve.wait_ge(v_hi, 2 * b + u + 1)
                            nc.vector.tensor_tensor(vst[:, u, :, 1, :], banks[u][:, :].rearrange("p (h d) -> p h d", h=HEADS),
                                                    f32(vst[:, u, :, 0, :]), ALU.subtract).then_inc(v_lo, 1)
                        else:
                            j = u - 2
                            dve.wait_ge(tanh_ok, 4 * b + j + 1)
                            if j >= 2 or not is_first(b):
                                dve.wait_ge(gate_out[j % 2], DMA * (2 * b + j // 2))
                            nc.vector.scalar_tensor_tensor(gate[:, j % 2, :, :], tanh[:, j % 2, :, :], 1.0,
                                                           banks[u][:, :].rearrange("p (c t) -> p c t", c=2),
                                                           ALU.add, ALU.mult).then_inc(gate_ok, 1)
                        if u in (0, 2, 4, 5) and nxt:
                            H.split_lo(dve, *nxt, (0, 2, 4, 5).index(u))
                        half = NTAP // 2
                        taps(i, s * half + u * half // UNITS, s * half + (u + 1) * half // UNITS)

            body(0, False)
            with dve.Fori(1, NBLK - 1) as i:
                body(i, False)
            body(NBLK - 1, True)

        @block.tensor
        def _(pe):
            for n in range(4):
                H.turn(pe, 0, 0, n, first=True)

            def body(i, last):
                for s in range(2):
                    b = 2 * i + s
                    nxt = None if last and s == 1 else (i + s, 1 - s)
                    pe.wait_ge(H.t_lo, 4 * (b + 1))
                    for u in range(UNITS):
                        if u == 0:
                            pe.wait_ge(W.w_lo, KT)
                        if u == 4:
                            pe.wait_ge(W.w_lo, 2 * KT)
                        if not is_first(b):
                            if u < 2:
                                pe.wait_ge(v_lo, 2 * b - 2 + u + 1)
                            else:
                                pe.wait_ge(gate_ok, 4 * b - 4 + (u - 2) + 1)
                        if u < 2:
                            w = slice(u * P, (u + 1) * P)
                            mm = product(nc, banks[u][:, :], lambda k: H.hi[s][:, k, w], lambda k: H.lo[s][:, k, w],
                                         lambda k: w_hi[:, k, 0:D_HALF], lambda k: w_lo[:, k, 0:D_HALF], KT)
                        else:
                            for c in range(2):
                                col = D_HALF + (2 * (u - 2) + c) * P
                                mm = product(nc, banks[u][:, c * SUB:(c + 1) * SUB],
                                             lambda k: w_hi[:, k, col:col + P], lambda k: w_lo[:, k, col:col + P],
                                             lambda k: H.hi[s][:, k, :], lambda k: H.lo[s][:, k, :], KT)
                        mm.then_inc(p_ps, 1)
                        if u in (0, 2, 4, 5) and nxt:
                            H.turn(pe, *nxt, (0, 2, 4, 5).index(u))

            body(0, False)
            with pe.Fori(1, NBLK - 1) as i:
                body(i, False)
            body(NBLK - 1, True)


def pass_3(nc, io, K, D):
    with ExitStack() as ctx:
        T = Tools(nc, ctx, "p3")
        raw = [T.sb(f"raw{j}", [P, D_MODEL]) for j in range(4)]
        W = Weights(nc, T, [r[:, :] for r in raw])
        pw_hi, pw_lo = T.sb("pw_hi", [P, CT, D_HALF], F32R), T.sb("pw_lo", [P, CT, D_HALF], F32R)
        wo_hi, wo_lo = T.sb("wo_hi", [P, CT, D_MODEL], F32R), T.sb("wo_lo", [P, CT, D_MODEL], F32R)
        for k in range(CT):
            W.add(io["w_pw"][0][k * P:(k + 1) * P, :], pw_hi[:, k, :], pw_lo[:, k, :])
        for k in range(CT):
            W.add(io["w_out"][0][D_HALF + k * P:D_HALF + (k + 1) * P, :], wo_hi[:, k, :], wo_lo[:, k, :])

        def tile4(name, dt=F32):
            return T.sb(name, [P, CT, BLK], dt)
        acc, dev, sq, gc = tile4("acc"), tile4("dev"), tile4("sq"), tile4("gc")
        hn, th, z, s_hi, s_lo = tile4("hn"), tile4("th"), tile4("z"), tile4("s_hi", F32R), tile4("s_lo", F32R)
        c4, c_hi, c_lo = tile4("c4"), tile4("c_hi", F32R), tile4("c_lo", F32R)
        sqs = T.sb("sqs", [P, 2, BLK])
        var_s, rstd = T.sb("var", [P, 4]), T.sb("rstd", [P, 4])
        yst = T.sb("yst", [P, 4, D_HALF])
        mean_b, var_b, rstd_b = T.bank("mean"), T.bank("varb"), T.bank("rstdb")
        pw_b = [T.bank(f"pw{j}") for j in range(2)]
        y_b = [T.bank(f"y{j}") for j in range(2)]
        acc_in, gc_in, y_out = T.sem("acc_in"), T.sem("gc_in"), T.sems("y_out", 4)
        mean_ps, dev_ok, sq_ok, sum_a, sum_ok = (T.sem(n) for n in ("mean_ps", "dev_ok", "sq_ok", "sum_a", "sum_ok"))
        var_ps, var_ok, rstd_ok, rstd_ps, hn_ok = (T.sem(n) for n in ("var_ps", "var_ok", "rstd_ok", "rstd_ps", "hn_ok"))
        th_ok, z_ok, s_ok, s_hi_ok, s_lo_ok = (T.sem(n) for n in ("th_ok", "z_ok", "s_ok", "s_hi_ok", "s_lo_ok"))
        pw_ps, c_ok, c_hi_ok, c_lo_ok, y_ps, y_ok = (T.sem(n) for n in ("pw_ps", "c_ok", "c_hi_ok", "c_lo_ok", "y_ps", "y_ok"))
        block = ctx.enter_context(nc.Block())
        YU = 8

        @block.sync
        def _(sp):
            acc_d = D["acc2"].rearrange("(c p) t -> p c t", p=P)
            gc_d = D["gc"].rearrange("(c p) t -> p c t", p=P)
            sp.dma_start(acc[:, :, :], acc_d[:, :, PAD:PAD + BLK]).then_inc(acc_in, DMA)
            sp.dma_start(gc[:, :, :], gc_d[:, :, PAD:PAD + BLK]).then_inc(gc_in, DMA)
            W.load(sp)
            sp.wait_ge(dev_ok, 1)
            sp.dma_start(acc[:, :, :], acc_d[:, :, PAD + BLK:PAD + 2 * BLK]).then_inc(acc_in, DMA)

            def body(i, left):
                if left >= 1:
                    sp.wait_ge(c_ok, CT * (i + 1))
                    sp.dma_start(gc[:, :, :], gc_d[:, :, bass.ds((i + 1) * BLK + PAD, BLK)]).then_inc(gc_in, DMA)
                if left >= 2:
                    sp.wait_ge(dev_ok, i + 2)
                    sp.dma_start(acc[:, :, :], acc_d[:, :, bass.ds((i + 2) * BLK + PAD, BLK)]).then_inc(acc_in, DMA)
                for u in range(YU):
                    sp.wait_ge(y_ok, YU * i + u + 1)
                    sp.dma_start(D["yc"][bass.ds(i * BLK + (u // 2) * P, P), (u % 2) * D_HALF:(u % 2 + 1) * D_HALF],
                                 yst[:, u % 4, :]).then_inc(y_out[u % 4], DMA)

            with sp.Fori(0, NBLK - 2) as i:
                body(i, 2)
            body(NBLK - 2, 1)
            body(NBLK - 1, 0)
            for j in range(4):
                sp.wait_ge(y_out[j], 2 * NBLK * DMA)


        @block.gpsimd
        def _(pool):
            def norm(i):
                pool.wait_ge(var_ps, i + 1)
                pool.wait_ge(var_ok, i + 1)
                nc.gpsimd.tensor_tensor(rstd[:, :], var_s[:, :], K["mhalf"][:, :], ALU.pow).then_inc(rstd_ok, 1)

            with pool.Fori(0, NBLK) as i:
                norm(i)

        @block.scalar
        def _(act):
            W.split_hi(act)

            def norm(i):
                act.wait_ge(dev_ok, i + 1)
                nc.scalar.activation(sq[:, :, :], dev[:, :, :], ACT.Square).then_inc(sq_ok, 1)

            def swish(i, c):
                if c == 0:
                    act.wait_ge(hn_ok, i + 1)
                nc.scalar.activation(th[:, c, :], hn[:, c, :], ACT.Tanh, scale=K["ln_gh"][:, c:c + 1],
                                     bias=K["ln_bh"][:, c:c + 1]).then_inc(th_ok, 1)
                nc.scalar.activation(z[:, c, :], hn[:, c, :], ACT.Identity, scale=K["ln_g"][:, c:c + 1],
                                     bias=K["ln_b"][:, c:c + 1]).then_inc(z_ok, 1)

            def swish_hi(i, c):
                act.wait_ge(s_ok, CT * i + c + 1)
                nc.scalar.activation(s_hi[:, c, :], z[:, c, :], ACT.Copy).then_inc(s_hi_ok, 1)

            def project_c(i):
                for c in range(CT):
                    act.wait_ge(c_ok, CT * i + c + 1)
                    nc.scalar.activation(c_hi[:, c, :], c4[:, c, :], ACT.Copy, scale=0.25).then_inc(c_hi_ok, 1)

            def y_units(i, u0, u1):
                for u in range(u0, u1):
                    act.wait_ge(y_ps, YU * i + u + 1)
                    if u >= 4 or not is_first(i):
                        act.wait_ge(y_out[u % 4], DMA * (2 * i + u // 4))
                    nc.scalar.activation(yst[:, u % 4, :], y_b[u % 2][:, :], ACT.Copy).then_inc(y_ok, 1)

            norm(0)
            for c in range(CT):
                swish(0, c)
            for c in range(CT):
                swish_hi(0, c)

            def body(i, last):
                if not last:
                    norm(i + 1)
                project_c(i)
                y_units(i, 0, 2)
                for c in range(CT):
                    if not last:
                        swish(i + 1, c)
                        if c > 0:
                            swish_hi(i + 1, c - 1)
                    y_units(i, 2 + c, 3 + c)
                if not last:
                    swish_hi(i + 1, CT - 1)
                y_units(i, 6, YU)

            body(0, False)
            with act.Fori(1, NBLK - 1) as i:
                body(i, False)
            body(NBLK - 1, True)

        @block.vector
        def _(dve):
            W.split_lo(dve)

            def norm(i):
                dve.wait_ge(acc_in, DMA * (i + 1))
                dve.wait_ge(mean_ps, i + 1)
                nc.vector.tensor_tensor(dev[:, :, :], acc[:, :, :], mean_b[:, None, :].broadcast_to([P, CT, BLK]),
                                        ALU.subtract).then_inc(dev_ok, 1)

            def var_sum(i):
                dve.wait_ge(sq_ok, i + 1)
                nc.vector.tensor_tensor(sqs[:, :, :], sq[:, 0:2, :], sq[:, 2:4, :], ALU.add).then_inc(sum_a, 1)
                dve.wait_ge(sum_a, i + 1)
                nc.vector.tensor_tensor(sq[:, 0, :], sqs[:, 0, :], sqs[:, 1, :], ALU.add).then_inc(sum_ok, 1)

            def var(i):
                dve.wait_ge(var_ps, i + 1)
                nc.vector.tensor_scalar(var_s[:, :], var_b[:, 0:4], EPS, None, ALU.add).then_inc(var_ok, 1)

            def swish(i):
                dve.wait_ge(rstd_ps, i + 1)
                nc.vector.tensor_tensor(hn[:, :, :], dev[:, :, :], rstd_b[:, None, :].broadcast_to([P, CT, BLK]),
                                        ALU.mult).then_inc(hn_ok, 1)

            def swish_s(i, c):
                dve.wait_ge(th_ok, CT * i + c + 1)
                dve.wait_ge(z_ok, CT * i + c + 1)
                nc.vector.scalar_tensor_tensor(z[:, c, :], th[:, c, :], 1.0, z[:, c, :], ALU.add, ALU.mult).then_inc(s_ok, 1)

            def swish_lo(i, c):
                dve.wait_ge(s_hi_ok, CT * i + c + 1)
                nc.vector.tensor_tensor(s_lo[:, c, :], z[:, c, :], f32(s_hi[:, c, :]), ALU.subtract).then_inc(s_lo_ok, 1)

            def swish_2(i):
                for c in range(CT + 1):
                    if c < CT:
                        swish_s(i, c)
                    if c > 0:
                        swish_lo(i, c - 1)

            def gate(i, c):
                if c == 0:
                    dve.wait_ge(gc_in, DMA * (i + 1))
                dve.wait_ge(pw_ps, CT * i + c + 1)
                nc.vector.scalar_tensor_tensor(c4[:, c, :], pw_b[c % 2][:, :], K["b_pw2"][:, c:c + 1], gc[:, c, :],
                                               ALU.add, ALU.mult).then_inc(c_ok, 1)

            def gate_lo(i, c):
                dve.wait_ge(c_hi_ok, CT * i + c + 1)
                nc.vector.scalar_tensor_tensor(c_lo[:, c, :], c4[:, c, :], 0.25, f32(c_hi[:, c, :]),
                                               ALU.mult, ALU.subtract).then_inc(c_lo_ok, 1)

            norm(0)
            var_sum(0)
            var(0)
            swish(0)
            swish_2(0)

            def body(i, last):
                if not last:
                    norm(i + 1)
                gate(i, 0)
                gate(i, 1)
                if not last:
                    var_sum(i + 1)
                gate_lo(i, 0)
                gate(i, 2)
                gate_lo(i, 1)
                gate_lo(i, 2)
                gate(i, 3)
                gate_lo(i, 3)
                if not last:
                    var(i + 1)
                    swish(i + 1)
                    swish_2(i + 1)

            with dve.Fori(0, NBLK - 1) as i:
                body(i, False)
            body(NBLK - 1, True)

        @block.tensor
        def _(pe):
            def mean(i, first=False):
                pe.wait_ge(acc_in, DMA * (i + 1))
                if not first:
                    pe.wait_ge(dev_ok, i)
                for c in range(CT):
                    mm = nc.tensor.matmul(mean_b[:, :], K["ones"][:, :], acc[:, c, :], start=(c == 0), stop=(c == CT - 1))
                mm.then_inc(mean_ps, 1)

            def variance(i, first=False):
                pe.wait_ge(sum_ok, i + 1)
                if not first:
                    pe.wait_ge(var_ok, i)
                for t in range(4):
                    mm = nc.tensor.matmul(var_b[:, t:t + 1], sq[:, 0, t * P:(t + 1) * P], K["ones"][:, 0:1], start=True, stop=True)
                mm.then_inc(var_ps, 1)

            def spread(i, first=False):
                pe.wait_ge(rstd_ok, i + 1)
                if not first:
                    pe.wait_ge(hn_ok, i)
                for t in range(4):
                    mm = nc.tensor.matmul(rstd_b[:, t * P:(t + 1) * P], rstd[:, t:t + 1].broadcast_to([P, P]), K["ident"][:, :],
                                          start=True, stop=True)
                mm.then_inc(rstd_ps, 1)

            def pointwise(i):
                for c in range(CT):
                    def swish_ready(k):
                        if c == 0:
                            pe.wait_ge(s_lo_ok, CT * i + k + 1)
                    if c >= 2 or not is_first(i):
                        pe.wait_ge(c_ok, CT * i + c - 1)
                    product(nc, pw_b[c % 2][:, :], lambda k: pw_hi[:, k, c * P:(c + 1) * P], lambda k: pw_lo[:, k, c * P:(c + 1) * P],
                            lambda k: s_hi[:, k, :], lambda k: s_lo[:, k, :], CT, before=swish_ready).then_inc(pw_ps, 1)

            def out_units(i, u0, u1):
                for u in range(u0, u1):
                    def branch_ready(k):
                        if u == 0:
                            pe.wait_ge(c_lo_ok, CT * i + k + 1)
                    if u >= 2 or not is_first(i):
                        pe.wait_ge(y_ok, YU * i + u - 1)
                    w, n = slice((u // 2) * P, (u // 2 + 1) * P), slice((u % 2) * D_HALF, (u % 2 + 1) * D_HALF)
                    product(nc, y_b[u % 2][:, :], lambda k: c_hi[:, k, w], lambda k: c_lo[:, k, w],
                            lambda k: wo_hi[:, k, n], lambda k: wo_lo[:, k, n], CT, before=branch_ready).then_inc(y_ps, 1)

            mean(0, True)
            variance(0, True)
            spread(0, True)
            pe.wait_ge(W.w_lo, 2 * CT)

            def body(i, last):
                if not last:
                    mean(i + 1)
                pointwise(i)
                if not last:
                    variance(i + 1)
                out_units(i, 0, 1)
                if not last:
                    spread(i + 1)
                out_units(i, 1, YU)

            body(0, False)
            with pe.Fori(1, NBLK - 1) as i:
                body(i, False)
            body(NBLK - 1, True)


def pass_4(nc, io, K, D, out):
    NG = SEQ // SUB
    WT = LEFT // P + 1
    RING = 8
    with ExitStack() as ctx:
        T = Tools(nc, ctx, "p4")
        ks = T.sb("ks", [P, HEADS, RING, P], F32R)
        vs = T.sb("vs", [P, RING, HEADS * P], F32R)
        q_hi, q_lo = (T.sb(n, [P, HEADS, SUB], F32R) for n in ("q_hi", "q_lo"))
        bias = T.sb("bias", [P, HEADS, WT * P])
        far = T.sb("far", [P, HEADS])
        pr = [T.sb(f"pr{t}", [P, WT * P]) for t in range(2)]
        pt_hi = [T.sb(f"pt_hi{j}", [P, WT + 1, SUB], F32R) for j in range(2)]
        pt_lo = [T.sb(f"pt_lo{j}", [P, WT + 1, SUB], F32R) for j in range(2)]
        wo_hi, wo_lo = T.sb("wo_hi", [P, CT, D_MODEL], F32R), T.sb("wo_lo", [P, CT, D_MODEL], F32R)
        ga = T.sb("ga", [P, CT, SUB])
        av, rg = T.sb("av", [P, CT, SUB]), T.sb("rg", [P, 2, SUB])
        a_hi, a_lo = T.sb("a_hi", [P, CT, SUB], F32R), T.sb("a_lo", [P, CT, SUB], F32R)
        low = T.sb("low", [P, SUB])
        y, x = T.sb("y", [P, 2, D_MODEL]), T.sb("x", [P, 2, D_MODEL])
        g_post = T.sb("g_post", [P, D_MODEL])
        junk = T.sb("junk", [P, D_HALF], BF16)
        nmax = T.sb("nmax", [P, 2 * HEADS])
        psum_ = [T.sb(f"psum{j}", [P, 2, HEADS]) for j in range(2)]
        rec, recx = T.sb("rec", [P, 2, HEADS]), T.sb("recx", [P, CT, SUB])
        ss, ms, mse, rstd = T.sb("ss", [P, 4]), T.sb("ms", [P, 2]), T.sb("mse", [P, 2]), T.sb("rstd", [P, 2])
        s_b, o_b, m_b = T.bank("s", 1024), T.bank("o"), T.bank("m")
        t_b = [T.bank(f"t{t}", 1024) for t in range(2)]
        W = Weights(nc, T, [x[:, 0, :], x[:, 1, :]])
        for k in range(CT):
            W.add(io["w_out"][0][k * P:(k + 1) * P, :], wo_hi[:, k, :], wo_lo[:, k, :])

        k_in, v_in, q_in = T.sems("k_in", 4), T.sems("v_in", 4), T.sems("q_in", 2)
        bias_in, bias_ok, far_in, post_in, zero_ok = (T.sem(n) for n in ("bias_in", "bias_ok", "far_in", "post_in", "zero_ok"))
        s_ps, max_ok, exp_ok, t_ps, hi_ok, lo_ok = (T.sem(n) for n in ("s_ps", "max_ok", "exp_ok", "t_ps", "hi_ok", "lo_ok"))
        o_ps, low_ok, av_ok = T.sem("o_ps"), T.sem("low_ok"), T.sem("av_ok")
        rec_ok, recx_ok, r_ps, m_read, gated, a_hi_ok, a_lo_ok, y_ps = (T.sem(n) for n in ("rec_ok", "recx_ok", "r_ps", "m_read", "gated", "a_hi_ok", "a_lo_ok", "y_ps"))
        max_begun, yg_ok = T.sem("max_begun"), T.sem("yg_ok")
        ga_in, yc_in, x_in, x_out = T.sem("ga_in"), T.sem("yc_in"), T.sem("x_in"), T.sem("x_out")
        ss_ok, ms_ok, rstd_ok, yn_ok, sum_ok = (T.sem(n) for n in ("ss_ok", "ms_ok", "rstd_ok", "yn_ok", "sum_ok"))
        block = ctx.enter_context(nc.Block())


        def tiles_of(g, t):
            first = max(t, 4 - 2 * g) if isinstance(g, int) else t
            return list(range(first, t + WT))

        def ring(slot, j):
            return (2 * slot + 4 + j) % RING

        def pieces(slot, js):
            r = [ring(slot, j) for j in js]

            def piece(p):
                if p == list(range(p[0], p[0] + len(p))):
                    return slice(p[0], p[0] + len(p))
                return slice(7, None, -7) if p == [7, 0] else None

            for n in ([len(r)] if len(r) <= 4 else []) + [3, 2]:
                both = [piece(x) for x in (r[:n], r[n:]) if x]
                if None not in both:
                    return both, n
            raise AssertionError(r)

        def all_groups(engine, body):
            for g in range(3):
                body(g, 0, g)
            with engine.Fori(0, (NG - 4) // 4) as r:
                for j in range(4):
                    body(4 * r + 3 + j, r + (3 + j) // 4, (3 + j) % 4)
            body(NG - 1, (NG - 1) // 4, (NG - 1) % 4)

        n_slots = 9
        Y_STEPS = [range(4 * CT * n // n_slots, 4 * CT * (n + 1) // n_slots) for n in range(n_slots)]
        Y_DONE = [[s // CT for s in Y_STEPS[n - 1] if s % CT == CT - 1] if n else [] for n in range(n_slots + 1)]

        def y_slot(h, t):
            n = 2 * (h - 2) + t
            return n if 0 <= n <= n_slots else None

        def is_last(g):
            return isinstance(g, int) and g == NG - 1

        @block.sync
        def _(sp):
            rows = "(h d) t -> d h t"

            def load_k(g, slot):
                for part in range(2):
                    sp.dma_start(f32(ks[part * HEAD_DIM:(part + 1) * HEAD_DIM, :, 2 * slot:2 * slot + 2, :]).rearrange("p h a t -> p h (a t)"),
                                 D["k"][part].rearrange(rows, d=HEAD_DIM)[:, :, bass.ds(g * SUB + PAD, SUB)]).then_inc(k_in[slot], DMA)

            def load_v(g, slot):
                sp.dma_start(f32(vs[:, 2 * slot:2 * slot + 2, :]),
                             D["v"][bass.ds(g * SUB, SUB), :].rearrange("(a p) c -> p a c", p=P)).then_inc(v_in[slot], DMA)

            def load_q(g, half):
                hs = slice(half * HEADS // 2, (half + 1) * HEADS // 2)
                for part, dst in ((0, q_hi), (1, q_lo)):
                    for top in range(2):
                        sp.dma_start(f32(dst[top * HEAD_DIM:(top + 1) * HEAD_DIM, hs, :]),
                                     D["q"][part].rearrange(rows, d=HEAD_DIM)[:, hs, bass.ds(g * SUB + PAD, SUB)]).then_inc(q_in[half], DMA)

            def load_ga(g):
                sp.dma_start(ga[:, :, :], D["ga"].rearrange("(c p) t -> p c t", p=P)[:, :, bass.ds(g * SUB + PAD, SUB)]).then_inc(ga_in, DMA)

            def load_yc(g):
                sp.dma_start(y[:, :, :], D["yc"][bass.ds(g * SUB, SUB), :].rearrange("(a p) d -> p a d", p=P)).then_inc(yc_in, DMA)

            def load_x(g):
                sp.dma_start(x[:, :, :], io["x"][0][bass.ds(g * SUB, SUB), :].rearrange("(a p) d -> p a d", p=P)).then_inc(x_in, DMA)

            def store(g):
                sp.wait_ge(sum_ok, 2 * (g + 1))
                sp.dma_start(out[0][bass.ds(g * SUB, SUB), :].rearrange("(a p) d -> p a d", p=P), x[:, :, :]).then_inc(x_out, DMA)

            copies, entries = D["rev"].shape[1:]
            near = bass.AP(D["rev"].tensor, P - 1, [[entries - 1, P], [copies * entries, HEADS], [1, 2 * P]])
            sp.dma_start(bias[:, :, 3 * P:], near).then_inc(bias_in, DMA)
            sp.dma_start(far[:, :], io["rel_bias"][0][:, 2 * MAX_REL].partition_broadcast(P),
                         allow_slow_non_contiguous=True).then_inc(far_in, DMA)
            load_q(0, 0)
            load_k(0, 0)
            load_q(0, 1)
            load_v(0, 0)
            load_k(1, 1)
            load_ga(0)
            sp.dma_start(g_post[:, :], io["post_norm_g"][0].partition_broadcast(P)).then_inc(post_in, DMA)
            load_yc(0)
            W.load(sp)
            sp.wait_ge(W.w_lo, CT)
            load_x(0)

            def body(g, quad, slot):
                if not is_first(g):
                    sp.wait_ge(o_ps, HEADS * g)
                    if not is_last(g):
                        load_k(g + 1, (slot + 1) % 4)
                if not is_last(g):
                    load_v(g + 1, (slot + 1) % 4)
                if not is_first(g):
                    sp.wait_ge(m_read, 6 * (g - 1) + 2)
                    load_ga(g)
                if not is_last(g):
                    for half in range(2):
                        sp.wait_ge(s_ps, 16 * g + 8 * (half + 1))
                        load_q(g + 1, half)
                if not is_first(g):
                    sp.wait_ge(sum_ok, 2 * g)
                    load_yc(g)
                    store(g - 1)
                    sp.wait_ge(x_out, DMA * g)
                    load_x(g)

            all_groups(sp, body)
            store(NG - 1)
            sp.wait_ge(x_out, DMA * NG)

        @block.gpsimd
        def _(pool):
            for j in range(2):
                for pt in (pt_hi, pt_lo):
                    for blind in (pt[j][:, 0, P:], pt[j][:, WT, 0:P]):
                        nc.gpsimd.tensor_tensor(blind, K["ident"][:, :], K["ident"][:, :], ALU.subtract).then_inc(zero_ok, 1)
            pool.wait_ge(zero_ok, 8)

            def branch(g):
                for part in range(2):
                    w = slice(2 * part, 2 * part + 2)
                    if part == 0:
                        pool.wait_ge(av_ok, HEADS * (g + 1))
                    pool.wait_ge(m_read, 6 * g + part + 1)
                    nc.gpsimd.tensor_tensor(av[:, w, :], av[:, w, :], rg[:, :, :], ALU.mult).then_inc(gated, 1)
                    pool.wait_ge(a_hi_ok, 2 * g + part + 1)
                    nc.gpsimd.tensor_tensor(a_lo[:, w, :], av[:, w, :], f32(a_hi[:, w, :]), ALU.subtract).then_inc(a_lo_ok, 1)

            def finish(g):
                pool.wait_ge(ss_ok, 4 * (g + 1))
                nc.gpsimd.tensor_tensor(ms[:, :], ss[:, 0:4:2], ss[:, 1:4:2], ALU.add).then_inc(ms_ok, 1)
                pool.wait_ge(ms_ok, 2 * g + 1)
                nc.gpsimd.tensor_tensor(mse[:, :], ms[:, :], K["eps"][:, 0:2], ALU.add).then_inc(ms_ok, 1)
                pool.wait_ge(ms_ok, 2 * g + 2)
                nc.gpsimd.tensor_tensor(rstd[:, :], mse[:, :], K["mhalf"][:, 0:2], ALU.pow).then_inc(rstd_ok, 1)
                for t in range(2):
                    if t == 0:
                        pool.wait_ge(x_in, DMA * (g + 1))
                    pool.wait_ge(yn_ok, 2 * g + t + 1)
                    nc.gpsimd.tensor_tensor(y[:, t, :], y[:, t, :], g_post[:, :], ALU.mult).then_inc(yg_ok, 1)
                    pool.wait_ge(yg_ok, 2 * g + t + 1)
                    nc.gpsimd.tensor_tensor(x[:, t, :], x[:, t, :], y[:, t, :], ALU.add).then_inc(sum_ok, 1)

            pool.wait_ge(post_in, DMA)
            with pool.Fori(0, NG) as g:
                branch(g)
                finish(g)

        @block.scalar
        def _(act):
            def exp(g, slot, h, t):
                n, w = 16 * g + 2 * h + t, len(tiles_of(g, t)) * P
                act.wait_ge(max_ok, n + 1)
                nc.scalar.activation(pr[t][:, 0:w], pr[t][:, 0:w], ACT.Exp, bias=nmax[:, 2 * h + t:2 * h + t + 1], scale=-1.0,
                                     accum_out=psum_[slot % 2][:, t, h:h + 1]).then_inc(exp_ok, 1)

            def hi(g, h, t):
                n, js = 16 * g + 2 * h + t, tiles_of(g, t)
                act.wait_ge(t_ps, n + 1)
                if not (is_first(g) and h < 2):
                    act.wait_ge(o_ps, HEADS * g + h - 1)
                nc.scalar.activation(pt_hi[h % 2][:, js[0]:js[-1] + 1, t * P:(t + 1) * P],
                                     t_b[t][:, 0:len(js) * P].rearrange("p (j q) -> p j q", q=P), ACT.Copy).then_inc(hi_ok, 1)

            def lower(g, h):
                o = (h % 2) * HEAD_DIM
                act.wait_ge(o_ps, HEADS * g + h + 1)
                if not (is_first(g) and h < 2):
                    act.wait_ge(av_ok, HEADS * g + h - 1)
                nc.scalar.activation(low[o:o + HEAD_DIM, :], o_b[HEAD_DIM:, 0:SUB], ACT.Copy).then_inc(low_ok, 1)

            def tail(g, part, t=None):
                if part in (0, 1):
                    act.wait_ge(gated, 2 * g + part + 1)
                    nc.scalar.activation(a_hi[:, 2 * part:2 * part + 2, :], av[:, 2 * part:2 * part + 2, :], ACT.Copy).then_inc(a_hi_ok, 1)
                elif part == "norm":
                    act.wait_ge(rstd_ok, g + 1)
                    nc.scalar.activation(y[:, t, :], y[:, t, :], ACT.Copy, scale=rstd[:, t:t + 1]).then_inc(yn_ok, 1)
                else:
                    u = part - 2
                    act.wait_ge(m_read, 6 * g + 2 + u + 1)
                    if not (is_first(g) and u == 0):
                        act.wait_ge(ss_ok, 4 * g + u)
                    nc.scalar.activation(junk[:, :], y[:, u // 2, (u % 2) * D_HALF:(u % 2 + 1) * D_HALF], ACT.Square,
                                         scale=D_MODEL ** -0.5, accum_out=ss[:, u:u + 1]).then_inc(ss_ok, 1)

            exp(0, 0, 0, 0)
            exp(0, 0, 0, 1)

            def body(g, quad, slot):
                for h in range(HEADS):
                    for t in range(2):
                        hi(g, h, t)
                        if t == 1 and not (is_first(g) and h == 0):
                            lower(g - (h == 0), (h - 1) % HEADS)
                        if h < HEADS - 1:
                            exp(g, slot, h + 1, t)
                        elif not is_last(g):
                            exp(g + 1, (slot + 1) % 4, 0, t)
                        if not is_first(g):
                            if (h, t) in ((1, 0), (2, 0)):
                                tail(g - 1, h - 1)
                            if y_slot(h, t) is not None:
                                for u in Y_DONE[y_slot(h, t)]:
                                    tail(g - 1, 2 + u)
                            if h == HEADS - 1:
                                tail(g - 1, "norm", t)
                    if is_first(g):
                        if h < CT:
                            W.split_hi(act, h, h + 1)

            all_groups(act, body)
            lower(NG - 1, HEADS - 1)
            for part in range(6):
                tail(NG - 1, part)
            for t in range(2):
                tail(NG - 1, "norm", t)

        @block.vector
        def _(dve):
            dve.wait_ge(bias_in, DMA)
            dve.wait_ge(far_in, DMA)
            nc.vector.tensor_copy(bias[:, :, 0:3 * P], far[:, :, None].broadcast_to([P, HEADS, 3 * P])).then_inc(bias_ok, 1)
            dve.wait_ge(bias_ok, 1)
            nc.vector.memset(bias[CHUNK:, :, 0:CHUNK], MASKED).then_inc(bias_ok, 1)
            nc.vector.memset(bias[0:CHUNK, :, WT * P - CHUNK:], MASKED).then_inc(bias_ok, 1)
            dve.wait_ge(bias_ok, 3)

            def maximum(g, slot, h, t):
                n, js = 16 * g + 2 * h + t, tiles_of(g, t)
                w, (both, n0) = len(js) * P, pieces(slot, js)
                o = 0 if len(both) == 1 else 512 - n0 * P
                dve.wait_ge(s_ps, n + 1)
                if not (is_first(g) and h == 0):
                    dve.wait_ge(t_ps, n - 1)
                dve.sem_inc(max_begun, 1)
                nc.vector.tensor_tensor_reduce(out=pr[t][:, 0:w], in0=s_b[:, o:o + w], in1=bias[:, h, WT * P - w:],
                                               scale=-1.0, scalar=3e38, op0=ALU.add, op1=ALU.min,
                                               accum_out=nmax[:, 2 * h + t:2 * h + t + 1]).then_inc(max_ok, 1)

            def lo(g, h, t):
                n, js = 16 * g + 2 * h + t, tiles_of(g, t)
                dst = slice(js[0], js[-1] + 1), slice(t * P, (t + 1) * P)
                dve.wait_ge(hi_ok, n + 1)
                nc.vector.tensor_tensor(pt_lo[h % 2][:, dst[0], dst[1]], t_b[t][:, 0:len(js) * P].rearrange("p (j q) -> p j q", q=P),
                                        f32(pt_hi[h % 2][:, dst[0], dst[1]]), ALU.subtract).then_inc(lo_ok, 1)

            def merge(g, h):
                o = (h % 2) * HEAD_DIM
                dve.wait_ge(low_ok, HEADS * g + h + 1)
                if h % 4 == 0 and not is_first(g):
                    dve.wait_ge(a_lo_ok, 2 * g - 1 + h // 4)
                nc.vector.tensor_tensor(av[o:o + HEAD_DIM, h // 2, :], o_b[0:HEAD_DIM, 0:SUB], low[o:o + HEAD_DIM, :],
                                        ALU.add).then_inc(av_ok, 1)

            def tail(g, slot, part):
                if part == "rec":
                    dve.wait_ge(exp_ok, 16 * (g + 1))
                    nc.vector.reciprocal(rec[:, :, :], psum_[slot % 2][:, :, :]).then_inc(rec_ok, 1)
                    dve.wait_ge(rec_ok, g + 1)
                    for half in range(2):
                        hs = slice(4 * half, 4 * half + 4)
                        nc.vector.tensor_scalar(recx[:, 2 * half:2 * half + 2, :].rearrange("p t (h d) -> p t h d", d=HEAD_DIM),
                                                rec[:, :, hs, None].broadcast_to([P, 2, 4, HEAD_DIM]), 0.5, None, ALU.mult).then_inc(recx_ok, 1)
                elif part in (0, 1):
                    w = slice(2 * part, 2 * part + 2)
                    dve.wait_ge(r_ps, 2 * g + part + 1)
                    if part == 0:
                        dve.wait_ge(ga_in, DMA * (g + 1))
                    if part > 0 or not is_first(g):
                        dve.wait_ge(gated, 2 * g + part)
                    nc.vector.tensor_tensor(rg[:, :, :], m_b[:, :].rearrange("p (c t) -> p c t", c=2), ga[:, w, :], ALU.mult).then_inc(m_read, 1)
                else:
                    u = part - 2
                    yv = y[:, u // 2, (u % 2) * D_HALF:(u % 2 + 1) * D_HALF]
                    dve.wait_ge(y_ps, 4 * g + u + 1)
                    if u == 0:
                        dve.wait_ge(yc_in, DMA * (g + 1))
                    nc.vector.tensor_tensor(yv, m_b[:, :], yv, ALU.add).then_inc(m_read, 1)

            maximum(0, 0, 0, 0)
            maximum(0, 0, 0, 1)

            def body(g, quad, slot):
                for h in range(HEADS):
                    if h == 0 and not is_first(g):
                        tail(g - 1, slot - 1, "rec")
                    for t in range(2):
                        if y_slot(h, t) is not None and not is_first(g):
                            for u in Y_DONE[y_slot(h, t)]:
                                tail(g - 1, slot - 1, 2 + u)
                        if h < HEADS - 1:
                            maximum(g, slot, h + 1, t)
                        elif not is_last(g):
                            maximum(g + 1, (slot + 1) % 4, 0, t)
                        lo(g, h, t)
                    if not (is_first(g) and h == 0):
                        merge(g - (h == 0), (h - 1) % HEADS)
                    if is_first(g):
                        if h < CT:
                            W.split_lo(dve, h, h + 1)
                    elif h < 2:
                        tail(g - 1, slot - 1, h)

            all_groups(dve, body)
            merge(NG - 1, HEADS - 1)
            for part in ("rec", 0, 1, 2, 3, 4, 5):
                tail(NG - 1, (NG - 1) % 4, part)

        @block.tensor
        def _(pe):
            def scores(g, quad, slot, h, t):
                n, js = 16 * g + 2 * h + t, tiles_of(g, t)
                both, n0 = pieces(slot, js)
                if h % 4 == 0 and t == 0:
                    pe.wait_ge(q_in[h // 4], 4 * DMA * (g + 1))
                if h == 0 and t == 0:
                    pe.wait_ge(k_in[slot], 2 * DMA * (quad + 1))
                if not (is_first(g) and h == 0 and t == 0):
                    pe.wait_ge(max_ok, n)
                o = 0 if len(both) == 1 else 512 - n0 * P
                for piece, count in zip(both, (n0, len(js) - n0)):
                    for part in (q_hi, q_lo):
                        mm = nc.tensor.matmul(s_b[:, o:o + count * P], part[:, h, t * P:(t + 1) * P], ks[:, h, piece, :],
                                              start=(part is q_hi), stop=(part is q_lo))
                    o += count * P
                mm.then_inc(s_ps, 1)

            def turn(g, h, t):
                n, js = 16 * g + 2 * h + t, tiles_of(g, t)
                pe.wait_ge(exp_ok, n + 1)
                if not (is_first(g) and h == 0):
                    pe.wait_ge(lo_ok, n - 1)
                for j in range(len(js)):
                    mm = nc.tensor.transpose(t_b[t][:, j * P:(j + 1) * P], pr[t][:, j * P:(j + 1) * P], K["ident"][:, :])
                mm.then_inc(t_ps, 1)

            def weigh(g, quad, slot, h, half):
                js = [j for j in range(WT + 1) if j in tiles_of(g, 0) + tiles_of(g, 1)]
                if half == 0:
                    pe.wait_ge(lo_ok, 16 * g + 2 * h + 2)
                    if h == 0:
                        pe.wait_ge(v_in[slot], DMA * (quad + 1))
                        if is_first(g):
                            pe.wait_ge(zero_ok, 8)
                    if not (is_first(g) and h == 0):
                        pe.wait_ge(av_ok, HEADS * g + h)
                for j in js[:len(js) // 2] if half == 0 else js[len(js) // 2:]:
                    for part in (pt_hi, pt_lo):
                        mm = nc.tensor.matmul(o_b[:, 0:SUB], vs[:, ring(slot, j), h * P:(h + 1) * P], part[h % 2][:, j, :],
                                              start=(j == js[0] and part is pt_hi), stop=(j == js[-1] and part is pt_lo))
                if half == 1:
                    mm.then_inc(o_ps, 1)

            def spread(g, part):
                pe.wait_ge(recx_ok, 2 * g + part + 1)
                if not (is_first(g) and part == 0):
                    pe.wait_ge(m_read, 6 * g + part)
                for pair in range(2):
                    for t in range(2):
                        mm = nc.tensor.matmul(m_b[:, pair * SUB + t * P:pair * SUB + (t + 1) * P],
                                              recx[:, 2 * part + t, pair * P:(pair + 1) * P], K["ident"][:, :],
                                              start=True, stop=True)
                mm.then_inc(r_ps, 1)

            def project(g, steps):
                for u, k in (divmod(s, CT) for s in steps):
                    if u == 0 and k % 2 == 0:
                        pe.wait_ge(a_lo_ok, 2 * g + k // 2 + 1)
                    if u == 0 and k == 0 and is_first(g):
                        pe.wait_ge(W.w_lo, CT)
                    if k == 0:
                        pe.wait_ge(m_read, 6 * g + 2 + u)
                    w, n = slice((u // 2) * P, (u // 2 + 1) * P), slice((u % 2) * D_HALF, (u % 2 + 1) * D_HALF)
                    nc.tensor.matmul(m_b[:, :], a_hi[:, k, w], wo_hi[:, k, n], start=(k == 0), stop=False)
                    nc.tensor.matmul(m_b[:, :], a_hi[:, k, w], wo_lo[:, k, n], start=False, stop=False)
                    mm = nc.tensor.matmul(m_b[:, :], a_lo[:, k, w], wo_hi[:, k, n], start=False, stop=(k == CT - 1))
                    if k == CT - 1:
                        mm.then_inc(y_ps, 1)

            scores(0, 0, 0, 0, 0)
            scores(0, 0, 0, 0, 1)

            def body(g, quad, slot):
                nxt = (g + 1, quad + (slot == 3), (slot + 1) % 4)
                for h in range(HEADS):
                    for t in range(2):
                        turn(g, h, t)
                        if h < HEADS - 1:
                            scores(g, quad, slot, h + 1, t)
                        elif not is_last(g):
                            scores(*nxt, 0, t)
                        if h > 0:
                            weigh(g, quad, slot, h - 1, t)
                        elif not is_first(g):
                            weigh(g - 1, quad - (slot == 0), (slot - 1) % 4, HEADS - 1, t)
                        if not is_first(g):
                            if h < 2 and t == 0:
                                spread(g - 1, h)
                            if y_slot(h, t) in range(n_slots):
                                project(g - 1, Y_STEPS[y_slot(h, t)])

            all_groups(pe, body)
            for half in range(2):
                weigh(NG - 1, (NG - 1) // 4, (NG - 1) % 4, HEADS - 1, half)
            for part in range(2):
                spread(NG - 1, part)
            project(NG - 1, range(4 * CT))


def build(nc, io, out):
    def scratch(name, shape, dt=F32):
        return nc.dram_tensor(name, shape, dt, kind="Internal").ap()

    D = {
        "q": scratch("q_parts", [2, D_HALF, PAD + SEQ]),
        "k": scratch("k_parts", [2, D_HALF, PAD + SEQ]),
        "v": scratch("v_parts", [SEQ, 2 * D_HALF]),
        "hg": scratch("glu", [D_HALF, PAD + SEQ]),
        "acc": scratch("conv_part", [D_HALF, PAD + SEQ]),
        "acc2": scratch("conv", [D_HALF, PAD + SEQ]),
        "ga": scratch("gate_att", [D_HALF, PAD + SEQ]),
        "gc": scratch("gate_conv", [D_HALF, PAD + SEQ]),
        "rev": scratch("rel_bias_reversed", [HEADS, P, 3 * P - 1]),
        "yc": scratch("y_conv", [SEQ, D_MODEL]),
    }
    with ExitStack() as ctx:
        T = Tools(nc, ctx, "k")
        K = {name: T.sb(name, [P, cols]) for name, cols in (
            ("ident", P), ("ones", P), ("eps", 4), ("mhalf", 4), ("g_pre", KT), ("dw_b", CT), ("ln_g", CT), ("ln_b", CT),
            ("b_pw", CT), ("ln_gh", CT), ("ln_bh", CT), ("b_pw2", CT), ("dwt", CT * TAPS))}
        setup(nc, io, K, D)
        pass_1(nc, io, K, D)
        pass_2(nc, io, K, D)
        pass_3(nc, io, K, D)
        pass_4(nc, io, K, D, out)


NAMES = ["x", "pre_norm_g", "w_in", "rel_bias", "dw_w", "dw_b", "conv_ln_g", "conv_ln_b", "w_pw", "b_pw", "w_out",
         "post_norm_g"]


def kernel(**inputs):
    import numpy as np
    import concourse.bacc as bacc
    from concourse.bass_utils import run_bass_kernel_spmd

    nc = bacc.Bacc("TRN2", target_bir_lowering=False, num_devices=1)
    arrays, io = {}, {}
    for name in NAMES:
        a = np.ascontiguousarray(inputs[name])
        arrays[f"in_{name}"] = a
        io[name] = nc.dram_tensor(f"in_{name}", a.shape, mybir.dt.from_np(a.dtype), kind="ExternalInput").ap()
    out = nc.dram_tensor("out", inputs["x"].shape, F32, kind="ExternalOutput").ap()
    build(nc, io, out)
    r = run_bass_kernel_spmd(nc, [arrays], core_ids=[0])
    return r.results[0]["out"]
```

```python
from contextlib import ExitStack

import concourse.bass as bass
from concourse import mybir

F32 = mybir.dt.float32
F32R = mybir.dt.float32r
BF16 = mybir.dt.bfloat16
ALU = mybir.AluOpType
ACT = mybir.ActivationFunctionType

P = 128
D_MODEL = 1024
SEQ = 4096
D_HALF = 512
HEADS = 8
HEAD_DIM = D_HALF // HEADS
CHUNK = 64
LEFT = 8 * CHUNK
MAX_REL = 128
TAPS = 31
HALO = TAPS - 1
PAD = 32
EPS = 1e-6
MASKED = -1e30

KT = D_MODEL // P
CT = D_HALF // P
SUB = 256
BLK = 512
NBLK = SEQ // BLK
DMA = 16
TAPS_1 = 14
TAPS_2 = TAPS - TAPS_1

COL_Q, COL_K, COL_V, COL_GA, COL_VAL, COL_GLU, COL_GC = (n * D_HALF for n in range(7))


def is_first(i):
    return isinstance(i, int) and i == 0


def f32(ap):
    return ap.bitcast(F32)


class Tools:

    def __init__(self, nc, ctx, tag):
        self.nc, self.ctx, self.tag = nc, ctx, tag

    def sb(self, name, shape, dt=F32):
        return self.ctx.enter_context(self.nc.sbuf_tensor(f"{self.tag}_{name}", shape, dt))

    def bank(self, name, cols=512):
        return self.ctx.enter_context(self.nc.psum_tensor(f"{self.tag}_{name}", [P, cols], F32))

    def sem(self, name):
        return self.ctx.enter_context(self.nc.semaphore(f"{self.tag}_{name}"))

    def sems(self, name, n):
        return [self.sem(f"{name}{j}") for j in range(n)]


def setup(nc, io, K, D):
    with ExitStack() as ctx:
        T = Tools(nc, ctx, "s")
        dw = T.sb("dw", [TAPS, D_HALF])
        ps = T.bank("ps")
        zeroed, ident_ok, loaded = T.sem("zeroed"), T.sem("ident_ok"), T.sem("loaded")
        dwt_ps, done, pdone = T.sem("dwt_ps"), T.sem("done"), T.sem("pdone")
        block = ctx.enter_context(nc.Block())

        @block.sync
        def _(sp):
            sp.dma_start(dw[:, :], io["dw_w"][0]).then_inc(loaded, DMA)
            for dst, src in ((K["g_pre"], "pre_norm_g"), (K["dw_b"], "dw_b"), (K["ln_g"], "conv_ln_g"),
                             (K["ln_b"], "conv_ln_b"), (K["b_pw"], "b_pw")):
                sp.dma_start(dst[:, :], io[src][0].rearrange("(t p) -> p t", p=P),
                             allow_slow_non_contiguous=True).then_inc(loaded, DMA)
            sp.wait_ge(loaded, 6 * DMA)

        @block.gpsimd
        def _(pool):
            nc.gpsimd.memset(K["ident"][:, :], 0.0).then_inc(zeroed, 1)
            nc.gpsimd.memset(K["eps"][:, :], EPS).then_inc(pdone, 1)
            nc.gpsimd.memset(K["mhalf"][:, :], -0.5).then_inc(pdone, 1)
            nc.gpsimd.memset(K["ones"][:, :], 1.0 / D_HALF).then_inc(pdone, 1)
            pool.wait_ge(zeroed, 1)
            nc.gpsimd.affine_select(out=K["ident"][:, :], in_=K["ident"][:, :], compare_op=ALU.not_equal,
                                    fill=1.0, base=0, pattern=[[-1, P]], channel_multiplier=1).then_inc(ident_ok, 1)
            pool.wait_ge(pdone, 3)

        @block.tensor
        def _(pe):
            pe.wait_ge(ident_ok, 1)
            pe.wait_ge(loaded, 6 * DMA)
            for c in range(CT):
                mm = nc.tensor.transpose(ps[:, c * TAPS:(c + 1) * TAPS], dw[:, c * P:(c + 1) * P],
                                         K["ident"][0:TAPS, 0:TAPS])
            mm.then_inc(dwt_ps, 1)

        @block.vector
        def _(dve):
            dve.wait_ge(loaded, 6 * DMA)
            nc.vector.tensor_scalar(K["ln_gh"][:, :], K["ln_g"][:, :], 0.5, None, ALU.mult).then_inc(done, 1)
            nc.vector.tensor_scalar(K["ln_bh"][:, :], K["ln_b"][:, :], 0.5, None, ALU.mult).then_inc(done, 1)
            nc.vector.tensor_scalar(K["b_pw2"][:, :], K["b_pw"][:, :], 2.0, None, ALU.mult).then_inc(done, 1)
            dve.wait_ge(dwt_ps, 1)
            nc.vector.tensor_scalar(K["dwt"][:, :], ps[:, 0:CT * TAPS], 0.5, None, ALU.mult).then_inc(done, 1)
            dve.wait_ge(done, 4)


class Hidden:

    def __init__(self, nc, T, K, x):
        self.nc, self.K, self.x = nc, K, x
        self.xb = [T.sb(f"x{s}", [P, 2, D_MODEL]) for s in range(2)]
        self.hi = [T.sb(f"hT_hi{s}", [P, KT, SUB], F32R) for s in range(2)]
        self.lo = [T.sb(f"hT_lo{s}", [P, KT, SUB], F32R) for s in range(2)]
        self.junk = T.sb("junk", [P, D_MODEL], BF16)
        self.ms = T.sb("ms", [P, 4])
        self.mse = T.sb("mse", [P, 4])
        self.rstd = T.sb("rstd", [P, 4])
        self.tb = [T.bank(f"tb{j}") for j in range(2)]
        self.x_in = T.sems("x_in", 2)
        self.squared, self.eps_added, self.rstd_ok = T.sem("squared"), T.sem("eps_added"), T.sem("rstd_ok")
        self.h_ok, self.t_ps, self.t_hi, self.t_lo = (T.sem(n) for n in ("h_ok", "t_ps", "t_hi", "t_lo"))

    def load(self, sp, i, s, block):
        rows = self.x[bass.ds((2 * block + s) * SUB, SUB), :]
        sp.dma_start(self.xb[s][:, :, :], rows.rearrange("(t p) d -> p t d", p=P)).then_inc(self.x_in[s], DMA)

    def square(self, act, i, s):
        act.wait_ge(self.x_in[s], DMA * (i + 1))
        for t in range(2):
            if t == 1:
                act.wait_ge(self.squared, 2 * (2 * i + s) + 1)
            self.nc.scalar.activation(self.junk[:, :], self.xb[s][:, t, :], ACT.Square, scale=D_MODEL ** -0.5,
                                      accum_out=self.ms[:, 2 * s + t:2 * s + t + 1]).then_inc(self.squared, 1)

    def power(self, pool, i, s):
        b = 2 * i + s
        w = slice(2 * s, 2 * s + 2)
        pool.wait_ge(self.squared, 2 * (b + 1))
        self.nc.gpsimd.tensor_tensor(self.mse[:, w], self.ms[:, w], self.K["eps"][:, 0:2], ALU.add).then_inc(self.eps_added, 1)
        pool.wait_ge(self.eps_added, b + 1)
        self.nc.gpsimd.tensor_tensor(self.rstd[:, w], self.mse[:, w], self.K["mhalf"][:, 0:2], ALU.pow).then_inc(self.rstd_ok, 1)

    def scale(self, dve, i, s):
        dve.wait_ge(self.rstd_ok, 2 * i + s + 1)
        for t in range(2):
            self.nc.vector.tensor_scalar(self.xb[s][:, t, :], self.xb[s][:, t, :],
                                         self.rstd[:, 2 * s + t:2 * s + t + 1], None, ALU.mult).then_inc(self.h_ok, 1)

    def turn(self, pe, i, s, n, first=False):
        b = 2 * i + s
        if n == 0:
            pe.wait_ge(self.h_ok, 2 * (b + 1))
        if not first or n >= 2:
            pe.wait_ge(self.t_lo, 4 * b + n - 1)
        for k in range(2):
            for t in range(2):
                mm = self.nc.tensor.transpose(self.tb[n % 2][:, k * SUB + t * P:k * SUB + (t + 1) * P],
                                              self.xb[s][:, t, (2 * n + k) * P:(2 * n + k + 1) * P],
                                              self.K["ident"][:, :])
        mm.then_inc(self.t_ps, 1)

    def split_hi(self, act, i, s, n):
        act.wait_ge(self.t_ps, 4 * (2 * i + s) + n + 1)
        self.nc.scalar.activation(self.hi[s][:, 2 * n:2 * n + 2, :], self.tb[n % 2][:, :].rearrange("p (k t) -> p k t", k=2),
                                  ACT.Copy).then_inc(self.t_hi, 1)

    def split_lo(self, dve, i, s, n):
        dve.wait_ge(self.t_hi, 4 * (2 * i + s) + n + 1)
        self.nc.vector.tensor_tensor(self.lo[s][:, 2 * n:2 * n + 2, :],
                                     self.tb[n % 2][:, :].rearrange("p (k t) -> p k t", k=2),
                                     f32(self.hi[s][:, 2 * n:2 * n + 2, :]), ALU.subtract).then_inc(self.t_lo, 1)


class Weights:

    def __init__(self, nc, T, raw):
        self.nc, self.raw, self.jobs = nc, raw, []
        self.raw_in = T.sems("raw_in", len(raw))
        self.w_hi, self.w_lo = T.sem("w_hi"), T.sem("w_lo")

    def add(self, src, hi, lo, gain=None, buf=None):
        self.jobs.append((src, hi, lo, gain, len(self.jobs) % len(self.raw) if buf is None else buf))

    def staged(self, n):
        src, *_, buf = self.jobs[n]
        return self.raw[buf][:, 0:src.shape[1]], buf, [m for m in range(n) if self.jobs[m][-1] == buf]

    def load(self, sp, n0=0, n1=None):
        for n in range(n0, len(self.jobs) if n1 is None else n1):
            raw, buf, before = self.staged(n)
            if before:
                sp.wait_ge(self.w_lo, before[-1] + 1)
            sp.dma_start(raw, self.jobs[n][0]).then_inc(self.raw_in[buf], DMA)

    def split_hi(self, act, n0=0, n1=None):
        for n in range(n0, len(self.jobs) if n1 is None else n1):
            _, hi, _, gain, _ = self.jobs[n]
            raw, buf, before = self.staged(n)
            act.wait_ge(self.raw_in[buf], DMA * (len(before) + 1))
            if gain is None:
                self.nc.scalar.activation(hi, raw, ACT.Copy).then_inc(self.w_hi, 1)
            else:
                self.nc.scalar.activation(hi, raw, ACT.Copy, scale=gain).then_inc(self.w_hi, 1)

    def split_lo(self, dve, n0=0, n1=None):
        for n in range(n0, len(self.jobs) if n1 is None else n1):
            _, hi, lo, gain, _ = self.jobs[n]
            raw, *_ = self.staged(n)
            dve.wait_ge(self.w_hi, n + 1)
            if gain is None:
                self.nc.vector.tensor_tensor(lo, raw, f32(hi), ALU.subtract).then_inc(self.w_lo, 1)
            else:
                self.nc.vector.scalar_tensor_tensor(lo, raw, gain, f32(hi), ALU.mult, ALU.subtract).then_inc(self.w_lo, 1)


def product(nc, out, stat_hi, stat_lo, mov_hi, mov_lo, tiles, before=None):
    for k in range(tiles):
        if before:
            before(k)
        nc.tensor.matmul(out, stat_hi(k), mov_hi(k), start=(k == 0), stop=False)
        nc.tensor.matmul(out, stat_hi(k), mov_lo(k), start=False, stop=False)
        mm = nc.tensor.matmul(out, stat_lo(k), mov_hi(k), start=False, stop=(k == tiles - 1))
    return mm


def pass_1(nc, io, K, D, H):
    w_in = io["w_in"][0]
    with ExitStack() as ctx:
        T = Tools(nc, ctx, "p1")
        GRP = 2 * D_HALF
        w_hi = [T.sb(f"w_hi{j}", [P, KT, GRP], F32R) for j in range(2)]
        w_lo = [T.sb(f"w_lo{j}", [P, KT, GRP], F32R) for j in range(2)]
        glu_t = T.sb("glu_t", [P, 2, SUB])
        hg = [T.sb(f"hg{s}", [P, CT, HALO + SUB]) for s in range(2)]
        acc = T.sb("acc", [P, CT, SUB])
        st = [T.sb(f"st{j}", [P, 2, 2, SUB], F32R) for j in range(2)]
        W = Weights(nc, T, [H.xb[1][:, 0, :], H.xb[1][:, 1, :],
                            *(acc[:, 2 * c:2 * c + 2, :].rearrange("p c t -> p (c t)") for c in range(2)),
                            *(f32(s[:, a, :, :]).rearrange("p c t -> p (c t)") for s in st for a in range(2))])
        for col, j, c0, bufs in ((COL_GLU, 0, D_HALF, (0, 1, 2, 3, 4, 5, 6, 7)), (COL_VAL, 0, 0, (2, 3, 4, 5, 6, 7, 2, 3)),
                                 (COL_Q, 1, 0, (4, 5, 6, 7, 2, 3, 4, 5)), (COL_K, 1, D_HALF, (6, 7, 4, 5, 6, 7, 4, 5))):
            for k in range(KT):
                W.add(w_in[k * P:(k + 1) * P, col:col + D_HALF], w_hi[j][:, k, c0:c0 + D_HALF], w_lo[j][:, k, c0:c0 + D_HALF],
                      K["g_pre"][:, k:k + 1], bufs[k])
        banks = [T.bank(f"pb{j}") for j in range(4)]
        free = T.sems("free", 4)
        p_ps = T.sem("p_ps")
        tanh_ok, hg_ok, halo_ok, tapped, hg_zero = (T.sem(n) for n in ("tanh_ok", "hg_ok", "halo_ok", "tapped", "hg_zero"))
        qk_hi, qk_lo = T.sem("qk_hi"), T.sem("qk_lo")
        zero_out = T.sem("zero_out")
        hg_out, acc_out, st_out = T.sems("hg_out", 2), T.sems("acc_out", 2), T.sems("st_out", 2)
        block = ctx.enter_context(nc.Block())

        UNITS = [(0, D_HALF), (0, 0), (0, D_HALF + 2 * P), (0, 2 * P),
                 (1, 0), (1, 2 * P), (1, D_HALF), (1, D_HALF + 2 * P)]
        NU = len(UNITS)
        NTAP = CT * TAPS_1

        @block.sync
        def _(sp):
            H.load(sp, 0, 0, 0)
            W.load(sp, 0, 12)
            sp.wait_ge(W.w_lo, 2)
            H.load(sp, 0, 1, 0)
            sp.wait_ge(hg_zero, 1)
            sp.dma_start(D["hg"].rearrange("(c p) t -> p c t", p=P)[:, :, PAD - HALO:PAD], hg[1][:, :, SUB:]).then_inc(zero_out, DMA)
            W.load(sp, 12)

            def body(i, last):
                for s in range(2):
                    b = 2 * i + s
                    cols = bass.ds(b * SUB + PAD, SUB)
                    sp.wait_ge(H.t_ps, 4 * (b + 1))
                    H.load(sp, i + 1, s, 0 if last else i + 1)
                    for pair in range(2):
                        sp.wait_ge(hg_ok, 2 * b + pair + 1)
                        sp.dma_start(D["hg"].rearrange("(c p) t -> p c t", p=P)[:, 2 * pair:2 * pair + 2, cols],
                                     hg[s][:, 2 * pair:2 * pair + 2, HALO:]).then_inc(hg_out[s], DMA)
                    for u in range(4):
                        if u == 2:
                            acc_store(b, cols, 0)
                        sp.wait_ge(qk_lo, 4 * b + u + 1)
                        dst = D["q" if u < 2 else "k"].rearrange("a (c p) t -> p a c t", p=P)
                        for part in range(2):
                            sp.dma_start(dst[:, part, 2 * (u % 2):2 * (u % 2) + 2, cols],
                                         f32(st[u % 2][:, part, :, :])).then_inc(st_out[u % 2], DMA)
                    acc_store(b, cols, 1)

            def acc_store(b, cols, pair):
                sp.wait_ge(tapped, NTAP * b + (pair + 1) * NTAP // 2)
                sp.dma_start(D["acc"].rearrange("(c p) t -> p c t", p=P)[:, 2 * pair:2 * pair + 2, cols],
                             acc[:, 2 * pair:2 * pair + 2, :]).then_inc(acc_out[pair], DMA)

            with sp.Fori(0, NBLK - 1) as i:
                body(i, False)
            body(NBLK - 1, True)
            for s in range(2):
                sp.wait_ge(hg_out[s], 2 * NBLK * DMA)
                sp.wait_ge(acc_out[s], 2 * NBLK * DMA)
                sp.wait_ge(st_out[s], 8 * NBLK * DMA)

        @block.gpsimd
        def _(pool):
            H.power(pool, 0, 0)

            def body(i, last):
                H.power(pool, i, 1)
                H.power(pool, i + 1, 0)

            with pool.Fori(0, NBLK - 1) as i:
                body(i, False)
            body(NBLK - 1, True)

        @block.scalar
        def _(act):
            H.square(act, 0, 0)
            for n in range(4):
                H.split_hi(act, 0, 0, n)
            W.split_hi(act, 0, KT + 4)

            def body(i, last):
                for s in range(2):
                    b = 2 * i + s
                    nxt = (i + s, 1 - s)
                    H.square(act, *nxt)
                    if is_first(b):
                        W.split_hi(act, KT + 4, 2 * KT)
                    for u in range(NU):
                        m = NU * b + u
                        if is_first(b) and u < 4:
                            W.split_hi(act, 2 * KT + 4 * u, 2 * KT + 4 * u + 4)
                        if u in (0, 2):
                            act.wait_ge(p_ps, m + 1)
                            if u > 0 or not is_first(b):
                                act.wait_ge(hg_ok, 2 * b + u // 2)
                            nc.scalar.activation(glu_t[:, :, :], banks[u % 4][:, :].rearrange("p (c t) -> p c t", c=2),
                                                 ACT.Tanh, scale=0.5).then_inc(tanh_ok, 1)
                        if u >= 4:
                            j = u - 4
                            if is_first(b) and u == 4:
                                act.wait_ge(W.w_lo, 4 * KT)
                            act.wait_ge(p_ps, m + 1)
                            if j >= 2 or not is_first(b):
                                act.wait_ge(st_out[j % 2], 2 * DMA * (2 * b + j // 2))
                            nc.scalar.activation(st[j % 2][:, 0, :, :], banks[u % 4][:, :].rearrange("p (c t) -> p c t", c=2),
                                                 ACT.Copy, scale=HEAD_DIM ** -0.5 if j < 2 else 1.0).then_inc(qk_hi, 1)
                        if u % 2 == 1:
                            H.split_hi(act, *nxt, u // 2)

            body(0, False)
            with act.Fori(1, NBLK - 1) as i:
                body(i, False)
            body(NBLK - 1, True)

        @block.vector
        def _(dve):
            nc.vector.memset(hg[1][:, :, SUB:], 0.0).then_inc(hg_zero, 1)
            H.scale(dve, 0, 0)
            for n in range(4):
                H.split_lo(dve, 0, 0, n)
            W.split_lo(dve, 0, KT + 4)
            dve.wait_ge(hg_zero, 1)

            def taps(b, s, n0, n1):
                for n in range(n0, n1):
                    pair, rest = divmod(n, 2 * TAPS_1)
                    tap, c = rest // 2, 2 * pair + rest % 2
                    if tap == 0:
                        if rest == 0:
                            dve.wait_ge(hg_ok, 2 * b + pair + 1)
                            dve.wait_ge(halo_ok, 2 * b + pair + 1)
                            if not is_first(b):
                                dve.wait_ge(acc_out[pair], DMA * b)
                        nc.vector.tensor_scalar(acc[:, c, :], hg[s][:, c, 0:SUB], K["dwt"][:, c * TAPS:c * TAPS + 1],
                                                K["dw_b"][:, c:c + 1], ALU.mult, ALU.add).then_inc(tapped, 1)
                    else:
                        dve.wait_ge(tapped, NTAP * b + n - 1)
                        nc.vector.scalar_tensor_tensor(acc[:, c, :], hg[s][:, c, tap:tap + SUB],
                                                       K["dwt"][:, c * TAPS + tap:c * TAPS + tap + 1], acc[:, c, :],
                                                       ALU.mult, ALU.add).then_inc(tapped, 1)

            def body(i, last):
                for s in range(2):
                    b = 2 * i + s
                    nxt = (i + s, 1 - s)
                    if is_first(b):
                        W.split_lo(dve, KT + 4, 2 * KT)
                    H.scale(dve, *nxt)
                    for pair in range(2):
                        w = slice(2 * pair, 2 * pair + 2)
                        if is_first(b):
                            W.split_lo(dve, (2 + pair) * KT, (3 + pair) * KT)
                        if pair == 0 and s == 1 and is_first(i):
                            dve.wait_ge(zero_out, DMA)
                        if pair == 0 and not is_first(i):
                            dve.wait_ge(hg_out[s], 2 * DMA * i)
                        if pair == 0 and not is_first(b):
                            dve.wait_ge(tapped, NTAP * b)
                        nc.vector.tensor_copy(hg[s][:, w, 0:HALO], hg[1 - s][:, w, SUB:]).then_inc(halo_ok, 1)
                        dve.wait_ge(tanh_ok, 2 * b + pair + 1)
                        dve.wait_ge(p_ps, NU * b + 2 * pair + 2)
                        nc.vector.scalar_tensor_tensor(hg[s][:, w, HALO:], glu_t[:, :, :], 1.0,
                                                       banks[2 * pair + 1][:, :].rearrange("p (c t) -> p c t", c=2),
                                                       ALU.add, ALU.mult).then_inc(hg_ok, 1)
                        H.split_lo(dve, *nxt, pair)
                        taps(b, s, pair * NTAP // 4, (pair + 1) * NTAP // 4)
                    for j in range(4):
                        u = 4 + j
                        dve.wait_ge(qk_hi, 4 * b + j + 1)
                        nc.vector.scalar_tensor_tensor(st[j % 2][:, 1, :, :], banks[u % 4][:, :].rearrange("p (c t) -> p c t", c=2),
                                                       HEAD_DIM ** -0.5 if j < 2 else 1.0, f32(st[j % 2][:, 0, :, :]),
                                                       ALU.mult, ALU.subtract).then_inc(qk_lo, 1)
                        if j % 2 == 1:
                            H.split_lo(dve, *nxt, 2 + j // 2)
                        taps(b, s, NTAP // 2 + j * NTAP // 8, NTAP // 2 + (j + 1) * NTAP // 8)

            body(0, False)
            with dve.Fori(1, NBLK - 1) as i:
                body(i, False)
            body(NBLK - 1, True)

        @block.tensor
        def _(pe):
            for n in range(4):
                H.turn(pe, 0, 0, n, first=True)

            def body(i, last):
                for s in range(2):
                    b = 2 * i + s
                    nxt = (i + s, 1 - s)
                    pe.wait_ge(H.t_lo, 4 * (b + 1))
                    for u, (j, col) in enumerate(UNITS):
                        def weights_ready(k):
                            if is_first(b) and u in (0, 1, 4, 6):
                                pe.wait_ge(W.w_lo, (0, 1, 4, 6).index(u) * KT + k + 1)
                        if u >= 4:
                            if u % 2 == 0:
                                pe.wait_ge(tanh_ok, 2 * b + (u - 4) // 2 + 1)
                            else:
                                pe.wait_ge(hg_ok, 2 * b + (u - 5) // 2 + 1)
                        else:
                            pe.wait_ge(qk_lo, 4 * b - 4 + u + 1) if not is_first(b) else None
                        for c in range(2):
                            mm = product(nc, banks[u % 4][:, c * SUB:(c + 1) * SUB],
                                         lambda k: w_hi[j][:, k, col + c * P:col + (c + 1) * P],
                                         lambda k: w_lo[j][:, k, col + c * P:col + (c + 1) * P],
                                         lambda k: H.hi[s][:, k, :], lambda k: H.lo[s][:, k, :], KT, before=weights_ready)
                        mm.then_inc(p_ps, 1)
                        if u % 2 == 1:
                            H.turn(pe, *nxt, u // 2)

            body(0, False)
            with pe.Fori(1, NBLK - 1) as i:
                body(i, False)
            body(NBLK - 1, True)


def pass_2(nc, io, K, D, H):
    w_in = io["w_in"][0]
    with ExitStack() as ctx:
        T = Tools(nc, ctx, "p2")
        GRP = 3 * D_HALF
        w_hi, w_lo = T.sb("w_hi", [P, KT, GRP], F32R), T.sb("w_lo", [P, KT, GRP], F32R)
        vst = T.sb("vst", [P, 2, HEADS, 2, HEAD_DIM], F32R)
        tanh = T.sb("tanh", [P, 2, 2, SUB])
        gate = T.sb("gate", [P, 2, 2, SUB])
        hgl = T.sb("hgl", [P, CT, HALO + BLK])
        acc = T.sb("acc", [P, CT, BLK])
        W = Weights(nc, T, [*(f32(vst[:, t, :, :, :]).rearrange("p h a d -> p (h a d)") for t in range(2)),
                            *(g[:, :, :, :].rearrange("p a c t -> p (a c t)") for g in (tanh, gate)),
                            acc[:, 2, :], acc[:, 3, :]])
        for j, (col, bufs) in enumerate(((COL_V, (0, 1, 2, 3, 4, 5, 0, 1)), (COL_GA, (2, 3, 4, 5, 0, 1, 2, 3)), (COL_GC, (4, 5) * 4))):
            w = slice(j * D_HALF, (j + 1) * D_HALF)
            for k in range(KT):
                W.add(w_in[k * P:(k + 1) * P, col:col + D_HALF], w_hi[:, k, w], w_lo[:, k, w], K["g_pre"][:, k:k + 1], bufs[k])
        banks = [T.bank(f"pb{j}") for j in range(6)]
        p_ps = T.sem("p_ps")
        v_hi, v_lo, tanh_ok, gate_ok, tapped = (T.sem(n) for n in ("v_hi", "v_lo", "tanh_ok", "gate_ok", "tapped"))
        v_out, gate_out = T.sem("v_out"), T.sems("gate_out", 2)
        hg_in, acc_in, acc_out = T.sems("hg_in", 2), T.sems("acc_in", 2), T.sems("acc_out", 2)
        block = ctx.enter_context(nc.Block())

        NTAP = CT * TAPS_2
        UNITS = 6
        TURNS = (0, 2, 4, 5)

        @block.sync
        def _(sp):
            W.load(sp, 0, 2 * KT)

            def conv_load(i, pair):
                w = slice(2 * pair, 2 * pair + 2)
                sp.dma_start(hgl[:, w, :], D["hg"].rearrange("(c p) t -> p c t", p=P)[:, w, bass.ds(i * BLK + PAD - HALO, HALO + BLK)]).then_inc(hg_in[pair], DMA)
                sp.dma_start(acc[:, w, :], D["acc"].rearrange("(c p) t -> p c t", p=P)[:, w, bass.ds(i * BLK + PAD, BLK)]).then_inc(acc_in[pair], DMA)

            conv_load(0, 0)
            W.load(sp, 2 * KT)

            def body(i, last):
                for s in range(2):
                    b = 2 * i + s
                    if not last:
                        sp.wait_ge(H.t_ps, 4 * (2 * NBLK + b + 1))
                        H.load(sp, NBLK + i + 1, s, i + 1)
                    sp.wait_ge(v_lo, 2 * (b + 1))
                    sp.dma_start(D["v"][bass.ds(b * SUB, SUB), :].rearrange("(t p) c -> p t c", p=P),
                                 f32(vst[:, :, :, :, :]).rearrange("p t h a d -> p t (h a d)")).then_inc(v_out, DMA)
                    for u in range(4):
                        sp.wait_ge(gate_ok, 4 * b + u + 1)
                        sp.dma_start(D["ga" if u < 2 else "gc"].rearrange("(c p) t -> p c t", p=P)[:, 2 * (u % 2):2 * (u % 2) + 2, bass.ds(b * SUB + PAD, SUB)],
                                     gate[:, u % 2, :, :]).then_inc(gate_out[u % 2], DMA)
                    if is_first(b):
                        sp.wait_ge(W.w_lo, 3 * KT)
                        conv_load(0, 1)
                    w = slice(2 * s, 2 * s + 2)
                    sp.wait_ge(tapped, NTAP * i + (s + 1) * NTAP // 2)
                    sp.dma_start(D["acc2"].rearrange("(c p) t -> p c t", p=P)[:, w, bass.ds(i * BLK + PAD, BLK)], acc[:, w, :]).then_inc(acc_out[s], DMA)
                    if not last:
                        sp.wait_ge(acc_out[s], DMA * (i + 1))
                        conv_load(i + 1, s)

            body(0, False)
            with sp.Fori(1, NBLK - 1) as i:
                body(i, False)
            body(NBLK - 1, True)
            sp.wait_ge(v_out, 2 * NBLK * DMA)
            for s in range(2):
                sp.wait_ge(gate_out[s], 4 * NBLK * DMA)
                sp.wait_ge(acc_out[s], NBLK * DMA)

        @block.gpsimd
        def _(pool):
            def body(i, last):
                H.power(pool, NBLK + i, 1)
                if not last:
                    H.power(pool, NBLK + i + 1, 0)

            with pool.Fori(0, NBLK - 1) as i:
                body(i, False)
            body(NBLK - 1, True)

        @block.scalar
        def _(act):
            def body(i, last):
                for s in range(2):
                    b = 2 * i + s
                    nxt = None if last and s == 1 else (NBLK + i + s, 1 - s)
                    if nxt:
                        H.square(act, *nxt)
                    if is_first(b):
                        W.split_hi(act, 0, 2 * KT)
                    for u in range(UNITS):
                        if is_first(b) and u < 4:
                            W.split_hi(act, 2 * KT + 2 * u, 2 * KT + 2 * u + 2)
                        if is_first(b) and u == 0:
                            act.wait_ge(W.w_lo, 2 * KT)
                        act.wait_ge(p_ps, UNITS * b + u + 1)
                        if u < 2:
                            if u == 0 and not is_first(b):
                                act.wait_ge(v_out, DMA * b)
                            nc.scalar.activation(vst[:, u, :, 0, :], banks[u][:, :].rearrange("p (h d) -> p h d", h=HEADS),
                                                 ACT.Copy).then_inc(v_hi, 1)
                        else:
                            j = u - 2
                            if j >= 2 or not is_first(b):
                                act.wait_ge(gate_ok, 4 * b + j - 1)
                            nc.scalar.activation(tanh[:, j % 2, :, :], banks[u][:, :].rearrange("p (c t) -> p c t", c=2),
                                                 ACT.Tanh, scale=0.5).then_inc(tanh_ok, 1)
                        if u in TURNS and nxt:
                            H.split_hi(act, *nxt, TURNS.index(u))

            body(0, False)
            with act.Fori(1, NBLK - 1) as i:
                body(i, False)
            body(NBLK - 1, True)

        @block.vector
        def _(dve):
            def taps(i, n0, n1):
                for n in range(n0, n1):
                    pair, rest = divmod(n, 2 * TAPS_2)
                    tap, c = TAPS_1 + rest // 2, 2 * pair + rest % 2
                    if rest == 0:
                        dve.wait_ge(hg_in[pair], DMA * (i + 1))
                        dve.wait_ge(acc_in[pair], DMA * (i + 1))
                    elif rest >= 2:
                        dve.wait_ge(tapped, NTAP * i + n - 1)
                    nc.vector.scalar_tensor_tensor(acc[:, c, :], hgl[:, c, tap:tap + BLK],
                                                   K["dwt"][:, c * TAPS + tap:c * TAPS + tap + 1], acc[:, c, :],
                                                   ALU.mult, ALU.add).then_inc(tapped, 1)

            def body(i, last):
                for s in range(2):
                    b = 2 * i + s
                    nxt = None if last and s == 1 else (NBLK + i + s, 1 - s)
                    if nxt:
                        H.scale(dve, *nxt)
                    if is_first(b):
                        W.split_lo(dve, 0, 2 * KT)
                    for u in range(UNITS):
                        if is_first(b) and u < 4:
                            W.split_lo(dve, 2 * KT + 2 * u, 2 * KT + 2 * u + 2)
                        if u < 2:
                            dve.wait_ge(v_hi, 2 * b + u + 1)
                            nc.vector.tensor_tensor(vst[:, u, :, 1, :], banks[u][:, :].rearrange("p (h d) -> p h d", h=HEADS),
                                                    f32(vst[:, u, :, 0, :]), ALU.subtract).then_inc(v_lo, 1)
                        else:
                            j = u - 2
                            dve.wait_ge(tanh_ok, 4 * b + j + 1)
                            if j >= 2 or not is_first(b):
                                dve.wait_ge(gate_out[j % 2], DMA * (2 * b + j // 2))
                            nc.vector.scalar_tensor_tensor(gate[:, j % 2, :, :], tanh[:, j % 2, :, :], 1.0,
                                                           banks[u][:, :].rearrange("p (c t) -> p c t", c=2),
                                                           ALU.add, ALU.mult).then_inc(gate_ok, 1)
                        if u in TURNS and nxt:
                            H.split_lo(dve, *nxt, TURNS.index(u))
                        half = NTAP // 2
                        taps(i, s * half + u * half // UNITS, s * half + (u + 1) * half // UNITS)

            body(0, False)
            with dve.Fori(1, NBLK - 1) as i:
                body(i, False)
            body(NBLK - 1, True)

        @block.tensor
        def _(pe):
            def body(i, last):
                for s in range(2):
                    b = 2 * i + s
                    nxt = None if last and s == 1 else (NBLK + i + s, 1 - s)
                    pe.wait_ge(H.t_lo, 4 * (2 * NBLK + b + 1))
                    for u in range(UNITS):
                        def weights_ready(k):
                            if is_first(b) and u in (0, 2, 4):
                                pe.wait_ge(W.w_lo, KT * (u // 2) + k + 1)
                        if not is_first(b):
                            if u < 2:
                                pe.wait_ge(v_lo, 2 * b - 2 + u + 1)
                            else:
                                pe.wait_ge(gate_ok, 4 * b - 4 + (u - 2) + 1)
                        if u < 2:
                            w = slice(u * P, (u + 1) * P)
                            mm = product(nc, banks[u][:, :], lambda k: H.hi[s][:, k, w], lambda k: H.lo[s][:, k, w],
                                         lambda k: w_hi[:, k, 0:D_HALF], lambda k: w_lo[:, k, 0:D_HALF], KT, before=weights_ready)
                        else:
                            for c in range(2):
                                col = D_HALF + (2 * (u - 2) + c) * P
                                mm = product(nc, banks[u][:, c * SUB:(c + 1) * SUB],
                                             lambda k: w_hi[:, k, col:col + P], lambda k: w_lo[:, k, col:col + P],
                                             lambda k: H.hi[s][:, k, :], lambda k: H.lo[s][:, k, :], KT, before=weights_ready)
                        mm.then_inc(p_ps, 1)
                        if u in TURNS and nxt:
                            H.turn(pe, *nxt, TURNS.index(u))

            body(0, False)
            with pe.Fori(1, NBLK - 1) as i:
                body(i, False)
            body(NBLK - 1, True)


def pass_3(nc, io, K, D):
    with ExitStack() as ctx:
        T = Tools(nc, ctx, "p3")
        raw = [T.sb(f"raw{j}", [P, D_MODEL]) for j in range(4)]
        W = Weights(nc, T, [r[:, :] for r in raw])
        pw_hi, pw_lo = T.sb("pw_hi", [P, CT, D_HALF], F32R), T.sb("pw_lo", [P, CT, D_HALF], F32R)
        wo_hi, wo_lo = T.sb("wo_hi", [P, CT, D_MODEL], F32R), T.sb("wo_lo", [P, CT, D_MODEL], F32R)
        for k in range(CT):
            W.add(io["w_pw"][0][k * P:(k + 1) * P, :], pw_hi[:, k, :], pw_lo[:, k, :])
        for k in range(CT):
            W.add(io["w_out"][0][D_HALF + k * P:D_HALF + (k + 1) * P, :], wo_hi[:, k, :], wo_lo[:, k, :])

        def tile4(name, dt=F32):
            return T.sb(name, [P, CT, BLK], dt)
        acc, dev, sq, gc = tile4("acc"), tile4("dev"), tile4("sq"), tile4("gc")
        hn, th, z, s_hi, s_lo = tile4("hn"), tile4("th"), tile4("z"), tile4("s_hi", F32R), tile4("s_lo", F32R)
        c4, c_hi, c_lo = tile4("c4"), tile4("c_hi", F32R), tile4("c_lo", F32R)
        sqs = T.sb("sqs", [P, 2, BLK])
        var_s, rstd = T.sb("var", [P, 4]), T.sb("rstd", [P, 4])
        yst = T.sb("yst", [P, 4, D_HALF])
        rel = T.sb("rel", [HEADS, 2 * MAX_REL + 1])
        rev = T.sb("rev", [HEADS, 3 * P - 1])
        rel_in, rev_ok, rev_out = T.sem("rel_in"), T.sem("rev_ok"), T.sem("rev_out")
        mean_b, var_b, rstd_b = T.bank("mean"), T.bank("varb"), T.bank("rstdb")
        pw_b = [T.bank(f"pw{j}") for j in range(2)]
        y_b = [T.bank(f"y{j}") for j in range(2)]
        acc_in, gc_in, y_out = T.sem("acc_in"), T.sem("gc_in"), T.sems("y_out", 4)
        mean_ps, dev_ok, sq_ok, sum_a, sum_ok = (T.sem(n) for n in ("mean_ps", "dev_ok", "sq_ok", "sum_a", "sum_ok"))
        var_ps, var_ok, rstd_ok, rstd_ps, hn_ok = (T.sem(n) for n in ("var_ps", "var_ok", "rstd_ok", "rstd_ps", "hn_ok"))
        th_ok, z_ok, s_ok, s_hi_ok, s_lo_ok = (T.sem(n) for n in ("th_ok", "z_ok", "s_ok", "s_hi_ok", "s_lo_ok"))
        pw_ps, c_ok, c_hi_ok, c_lo_ok, y_ps, y_ok = (T.sem(n) for n in ("pw_ps", "c_ok", "c_hi_ok", "c_lo_ok", "y_ps", "y_ok"))
        block = ctx.enter_context(nc.Block())
        YU = 8

        @block.sync
        def _(sp):
            acc_d = D["acc2"].rearrange("(c p) t -> p c t", p=P)
            gc_d = D["gc"].rearrange("(c p) t -> p c t", p=P)
            sp.dma_start(acc[:, :, :], acc_d[:, :, PAD:PAD + BLK]).then_inc(acc_in, DMA)
            sp.dma_start(gc[:, :, :], gc_d[:, :, PAD:PAD + BLK]).then_inc(gc_in, DMA)
            W.load(sp)
            sp.dma_start(rel[:, :], io["rel_bias"][0]).then_inc(rel_in, DMA)
            sp.wait_ge(dev_ok, 1)
            sp.dma_start(acc[:, :, :], acc_d[:, :, PAD + BLK:PAD + 2 * BLK]).then_inc(acc_in, DMA)

            def body(i, left):
                if left >= 1:
                    sp.wait_ge(c_ok, CT * (i + 1))
                    sp.dma_start(gc[:, :, :], gc_d[:, :, bass.ds((i + 1) * BLK + PAD, BLK)]).then_inc(gc_in, DMA)
                if left >= 2:
                    sp.wait_ge(dev_ok, i + 2)
                    sp.dma_start(acc[:, :, :], acc_d[:, :, bass.ds((i + 2) * BLK + PAD, BLK)]).then_inc(acc_in, DMA)
                for u in range(YU):
                    sp.wait_ge(y_ok, YU * i + u + 1)
                    sp.dma_start(D["yc"][bass.ds(i * BLK + (u // 2) * P, P), (u % 2) * D_HALF:(u % 2 + 1) * D_HALF],
                                 yst[:, u % 4, :]).then_inc(y_out[u % 4], DMA)

            body(0, 2)
            sp.wait_ge(rev_ok, 2)
            sp.dma_start(D["rev"], rev[:, None, :].broadcast_to([HEADS, P, 3 * P - 1])).then_inc(rev_out, DMA)
            with sp.Fori(1, NBLK - 2) as i:
                body(i, 2)
            body(NBLK - 2, 1)
            body(NBLK - 1, 0)
            for j in range(4):
                sp.wait_ge(y_out[j], 2 * NBLK * DMA)
            sp.wait_ge(rev_out, DMA)


        @block.gpsimd
        def _(pool):
            def norm(i):
                pool.wait_ge(var_ps, i + 1)
                pool.wait_ge(var_ok, i + 1)
                nc.gpsimd.tensor_tensor(rstd[:, :], var_s[:, :], K["mhalf"][:, :], ALU.pow).then_inc(rstd_ok, 1)

            with pool.Fori(0, NBLK) as i:
                norm(i)

        @block.scalar
        def _(act):
            def norm(i):
                act.wait_ge(dev_ok, i + 1)
                nc.scalar.activation(sq[:, :, :], dev[:, :, :], ACT.Square).then_inc(sq_ok, 1)

            def swish(i, c):
                act.wait_ge(hn_ok, CT * i + c + 1)
                nc.scalar.activation(th[:, c, :], hn[:, c, :], ACT.Tanh, scale=K["ln_gh"][:, c:c + 1],
                                     bias=K["ln_bh"][:, c:c + 1]).then_inc(th_ok, 1)
                nc.scalar.activation(z[:, c, :], hn[:, c, :], ACT.Identity, scale=K["ln_g"][:, c:c + 1],
                                     bias=K["ln_b"][:, c:c + 1]).then_inc(z_ok, 1)

            def swish_hi(i, c):
                act.wait_ge(s_ok, CT * i + c + 1)
                nc.scalar.activation(s_hi[:, c, :], z[:, c, :], ACT.Copy).then_inc(s_hi_ok, 1)

            def project_c(i):
                for c in range(CT):
                    act.wait_ge(c_ok, CT * i + c + 1)
                    nc.scalar.activation(c_hi[:, c, :], c4[:, c, :], ACT.Copy, scale=0.25).then_inc(c_hi_ok, 1)

            def y_units(i, u0, u1):
                for u in range(u0, u1):
                    act.wait_ge(y_ps, YU * i + u + 1)
                    if u >= 4 or not is_first(i):
                        act.wait_ge(y_out[u % 4], DMA * (2 * i + u // 4))
                    nc.scalar.activation(yst[:, u % 4, :], y_b[u % 2][:, :], ACT.Copy).then_inc(y_ok, 1)

            W.split_hi(act, 0, 2)
            norm(0)
            W.split_hi(act, 2)
            for c in range(CT):
                swish(0, c)
                if c > 0:
                    swish_hi(0, c - 1)
            swish_hi(0, CT - 1)

            def body(i, last):
                if not last:
                    norm(i + 1)
                project_c(i)
                y_units(i, 0, 2)
                for c in range(CT):
                    if not last:
                        swish(i + 1, c)
                        if c > 0:
                            swish_hi(i + 1, c - 1)
                    y_units(i, 2 + c, 3 + c)
                if not last:
                    swish_hi(i + 1, CT - 1)
                y_units(i, 6, YU)

            body(0, False)
            with act.Fori(1, NBLK - 1) as i:
                body(i, False)
            body(NBLK - 1, True)

        @block.vector
        def _(dve):
            def norm(i):
                dve.wait_ge(acc_in, DMA * (i + 1))
                dve.wait_ge(mean_ps, i + 1)
                nc.vector.tensor_tensor(dev[:, :, :], acc[:, :, :], mean_b[:, None, :].broadcast_to([P, CT, BLK]),
                                        ALU.subtract).then_inc(dev_ok, 1)

            def var_sum(i):
                dve.wait_ge(sq_ok, i + 1)
                nc.vector.tensor_tensor(sqs[:, :, :], sq[:, 0:2, :], sq[:, 2:4, :], ALU.add).then_inc(sum_a, 1)
                dve.wait_ge(sum_a, i + 1)
                nc.vector.tensor_tensor(sq[:, 0, :], sqs[:, 0, :], sqs[:, 1, :], ALU.add).then_inc(sum_ok, 1)

            def var(i):
                dve.wait_ge(var_ps, i + 1)
                nc.vector.tensor_scalar(var_s[:, :], var_b[:, 0:4], EPS, None, ALU.add).then_inc(var_ok, 1)

            def swish(i):
                dve.wait_ge(rstd_ps, i + 1)
                for c in range(CT):
                    nc.vector.tensor_tensor(hn[:, c, :], dev[:, c, :], rstd_b[:, :], ALU.mult).then_inc(hn_ok, 1)

            def swish_s(i, c):
                dve.wait_ge(th_ok, CT * i + c + 1)
                dve.wait_ge(z_ok, CT * i + c + 1)
                nc.vector.scalar_tensor_tensor(z[:, c, :], th[:, c, :], 1.0, z[:, c, :], ALU.add, ALU.mult).then_inc(s_ok, 1)

            def swish_lo(i, c):
                dve.wait_ge(s_hi_ok, CT * i + c + 1)
                nc.vector.tensor_tensor(s_lo[:, c, :], z[:, c, :], f32(s_hi[:, c, :]), ALU.subtract).then_inc(s_lo_ok, 1)

            def swish_2(i):
                for c in range(CT + 1):
                    if c < CT:
                        swish_s(i, c)
                    if c > 0:
                        swish_lo(i, c - 1)

            def gate(i, c):
                if c == 0:
                    dve.wait_ge(gc_in, DMA * (i + 1))
                dve.wait_ge(pw_ps, CT * i + c + 1)
                nc.vector.scalar_tensor_tensor(c4[:, c, :], pw_b[c % 2][:, :], K["b_pw2"][:, c:c + 1], gc[:, c, :],
                                               ALU.add, ALU.mult).then_inc(c_ok, 1)

            def gate_lo(i, c):
                dve.wait_ge(c_hi_ok, CT * i + c + 1)
                nc.vector.scalar_tensor_tensor(c_lo[:, c, :], c4[:, c, :], 0.25, f32(c_hi[:, c, :]),
                                               ALU.mult, ALU.subtract).then_inc(c_lo_ok, 1)

            W.split_lo(dve, 0, 2)
            norm(0)
            W.split_lo(dve, 2, 3)
            var_sum(0)
            W.split_lo(dve, 3, 4)
            var(0)
            W.split_lo(dve, 4, 5)
            swish(0)
            W.split_lo(dve, 5)
            swish_2(0)
            dve.wait_ge(rel_in, DMA)
            nc.vector.tensor_copy(rev[:, 0:P - 1], rel[:, 2 * MAX_REL:].broadcast_to([HEADS, P - 1])).then_inc(rev_ok, 1)
            nc.vector.tensor_copy(rev[:, P - 1:], rel[:, 2 * MAX_REL:0:-1]).then_inc(rev_ok, 1)

            def body(i, last):
                if not last:
                    norm(i + 1)
                gate(i, 0)
                gate(i, 1)
                if not last:
                    var_sum(i + 1)
                gate_lo(i, 0)
                gate(i, 2)
                gate_lo(i, 1)
                gate_lo(i, 2)
                gate(i, 3)
                gate_lo(i, 3)
                if not last:
                    var(i + 1)
                    swish(i + 1)
                    swish_2(i + 1)

            with dve.Fori(0, NBLK - 1) as i:
                body(i, False)
            body(NBLK - 1, True)

        @block.tensor
        def _(pe):
            def mean(i, first=False):
                pe.wait_ge(acc_in, DMA * (i + 1))
                if not first:
                    pe.wait_ge(dev_ok, i)
                for c in range(CT):
                    mm = nc.tensor.matmul(mean_b[:, :], K["ones"][:, :], acc[:, c, :], start=(c == 0), stop=(c == CT - 1))
                mm.then_inc(mean_ps, 1)

            def variance(i, first=False):
                pe.wait_ge(sum_ok, i + 1)
                if not first:
                    pe.wait_ge(var_ok, i)
                for t in range(4):
                    mm = nc.tensor.matmul(var_b[:, t:t + 1], sq[:, 0, t * P:(t + 1) * P], K["ones"][:, 0:1], start=True, stop=True)
                mm.then_inc(var_ps, 1)

            def spread(i, first=False):
                pe.wait_ge(rstd_ok, i + 1)
                if not first:
                    pe.wait_ge(hn_ok, CT * i)
                for t in range(4):
                    mm = nc.tensor.matmul(rstd_b[:, t * P:(t + 1) * P], rstd[:, t:t + 1].broadcast_to([P, P]), K["ident"][:, :],
                                          start=True, stop=True)
                mm.then_inc(rstd_ps, 1)

            def pointwise(i):
                for c in range(CT):
                    def swish_ready(k):
                        if c == 0:
                            pe.wait_ge(s_lo_ok, CT * i + k + 1)
                    if c >= 2 or not is_first(i):
                        pe.wait_ge(c_ok, CT * i + c - 1)
                    product(nc, pw_b[c % 2][:, :], lambda k: pw_hi[:, k, c * P:(c + 1) * P], lambda k: pw_lo[:, k, c * P:(c + 1) * P],
                            lambda k: s_hi[:, k, :], lambda k: s_lo[:, k, :], CT, before=swish_ready).then_inc(pw_ps, 1)

            def out_units(i, u0, u1):
                for u in range(u0, u1):
                    if u == 0 and is_first(i):
                        pe.wait_ge(W.w_lo, 2 * CT)

                    def branch_ready(k):
                        if u == 0:
                            pe.wait_ge(c_lo_ok, CT * i + k + 1)
                    if u >= 2 or not is_first(i):
                        pe.wait_ge(y_ok, YU * i + u - 1)
                    w, n = slice((u // 2) * P, (u // 2 + 1) * P), slice((u % 2) * D_HALF, (u % 2 + 1) * D_HALF)
                    product(nc, y_b[u % 2][:, :], lambda k: c_hi[:, k, w], lambda k: c_lo[:, k, w],
                            lambda k: wo_hi[:, k, n], lambda k: wo_lo[:, k, n], CT, before=branch_ready).then_inc(y_ps, 1)

            mean(0, True)
            variance(0, True)
            spread(0, True)
            pe.wait_ge(W.w_lo, CT)

            def body(i, last):
                if not last:
                    mean(i + 1)
                pointwise(i)
                if not last:
                    variance(i + 1)
                out_units(i, 0, 1)
                if not last:
                    spread(i + 1)
                out_units(i, 1, YU)

            body(0, False)
            with pe.Fori(1, NBLK - 1) as i:
                body(i, False)
            body(NBLK - 1, True)


def pass_4(nc, io, K, D, out):
    NG = SEQ // SUB
    WT = LEFT // P + 1
    RING = 8
    with ExitStack() as ctx:
        T = Tools(nc, ctx, "p4")
        ks = T.sb("ks", [P, HEADS, RING, P], F32R)
        vs = T.sb("vs", [P, RING, HEADS * P], F32R)
        q_hi, q_lo = (T.sb(n, [P, HEADS, SUB], F32R) for n in ("q_hi", "q_lo"))
        bias = T.sb("bias", [P, HEADS, WT * P])
        far = T.sb("far", [P, HEADS])
        pr = [T.sb(f"pr{t}", [P, WT * P]) for t in range(2)]
        pt_hi = [T.sb(f"pt_hi{j}", [P, WT + 1, SUB], F32R) for j in range(2)]
        pt_lo = [T.sb(f"pt_lo{j}", [P, WT + 1, SUB], F32R) for j in range(2)]
        wo_hi, wo_lo = T.sb("wo_hi", [P, CT, D_MODEL], F32R), T.sb("wo_lo", [P, CT, D_MODEL], F32R)
        ga = T.sb("ga", [P, CT, SUB])
        av, rg = T.sb("av", [P, CT, SUB]), T.sb("rg", [P, 2, SUB])
        a_hi, a_lo = T.sb("a_hi", [P, CT, SUB], F32R), T.sb("a_lo", [P, CT, SUB], F32R)
        low = T.sb("low", [P, SUB])
        y, x = T.sb("y", [P, 2, D_MODEL]), T.sb("x", [P, 2, D_MODEL])
        g_post = T.sb("g_post", [P, D_MODEL])
        junk = T.sb("junk", [P, D_HALF], BF16)
        nmax = T.sb("nmax", [P, 2 * HEADS])
        psum_ = [T.sb(f"psum{j}", [P, 2, HEADS]) for j in range(2)]
        rec, recx = T.sb("rec", [P, 2, HEADS]), T.sb("recx", [P, CT, SUB])
        ss, ms, mse, rstd = T.sb("ss", [P, 4]), T.sb("ms", [P, 2]), T.sb("mse", [P, 2]), T.sb("rstd", [P, 2])
        s_b, o_b, m_b = T.bank("s", 1024), T.bank("o"), T.bank("m")
        t_b = [T.bank(f"t{t}", 1024) for t in range(2)]
        W = Weights(nc, T, [x[:, 0, :], x[:, 1, :]])
        for k in range(CT):
            W.add(io["w_out"][0][k * P:(k + 1) * P, :], wo_hi[:, k, :], wo_lo[:, k, :])

        k_in, v_in, q_in = T.sems("k_in", 2), T.sems("v_in", 2), T.sems("q_in", 2)
        bias_in, bias_ok, far_in, post_in, zero_ok = (T.sem(n) for n in ("bias_in", "bias_ok", "far_in", "post_in", "zero_ok"))
        s_ps, max_ok, exp_ok, t_ps, hi_ok, lo_ok = (T.sem(n) for n in ("s_ps", "max_ok", "exp_ok", "t_ps", "hi_ok", "lo_ok"))
        o_ps, low_ok, av_ok = T.sem("o_ps"), T.sem("low_ok"), T.sem("av_ok")
        rec_ok, recx_ok, r_ps, m_read, gated, a_hi_ok, a_lo_ok, y_ps = (T.sem(n) for n in ("rec_ok", "recx_ok", "r_ps", "m_read", "gated", "a_hi_ok", "a_lo_ok", "y_ps"))
        max_begun, yg_ok = T.sem("max_begun"), T.sem("yg_ok")
        ga_in, yc_in, x_in, x_out = T.sem("ga_in"), T.sem("yc_in"), T.sem("x_in"), T.sem("x_out")
        ss_ok, ms_ok, rstd_ok, yn_ok, sum_ok = (T.sem(n) for n in ("ss_ok", "ms_ok", "rstd_ok", "yn_ok", "sum_ok"))
        block = ctx.enter_context(nc.Block())


        def tiles_of(g, t):
            first = max(t, 4 - 2 * g) if isinstance(g, int) else t
            return list(range(first, t + WT))

        def ring(slot, j):
            return (2 * slot + 4 + j) % RING

        def pieces(slot, js):
            r = [ring(slot, j) for j in js]

            def piece(p):
                if p == list(range(p[0], p[0] + len(p))):
                    return slice(p[0], p[0] + len(p))
                return slice(7, None, -7) if p == [7, 0] else None

            for n in ([len(r)] if len(r) <= 4 else []) + [3, 2]:
                both = [piece(x) for x in (r[:n], r[n:]) if x]
                if None not in both:
                    return both, n
            raise AssertionError(r)

        def all_groups(engine, body):
            for g in range(3):
                body(g, 0, g)
            with engine.Fori(0, (NG - 4) // 4) as r:
                for j in range(4):
                    body(4 * r + 3 + j, r + (3 + j) // 4, (3 + j) % 4)
            body(NG - 1, (NG - 1) // 4, (NG - 1) % 4)

        n_slots = 8
        Y_STEPS = [range(4 * CT * n // n_slots, 4 * CT * (n + 1) // n_slots) for n in range(n_slots)]
        Y_DONE = [[s // CT for s in Y_STEPS[n - 1] if s % CT == CT - 1] if n else [] for n in range(n_slots + 1)]

        def y_bank(g, u):
            return (m_b[:, :], s_b[:, 0:512], s_b[:, 512:], t_b[0][:, 0:512])[u] if is_last(g) else m_b[:, :]

        def o_bank(h):
            return m_b[:, 0:SUB] if h == HEADS - 2 else o_b[:, 0:SUB]

        def y_slot(h, t):
            n = 2 * (h - 2) + t - 1
            return n if 0 <= n <= n_slots else None

        def is_last(g):
            return isinstance(g, int) and g == NG - 1

        rows = "(h d) t -> d h t"

        def load_q(engine, g, half):
            hs = slice(half * HEADS // 2, (half + 1) * HEADS // 2)
            for part, dst in ((0, q_hi), (1, q_lo)):
                for top in range(2):
                    engine.dma_start(f32(dst[top * HEAD_DIM:(top + 1) * HEAD_DIM, hs, :]),
                                     D["q"][part].rearrange(rows, d=HEAD_DIM)[:, hs, bass.ds(g * SUB + PAD, SUB)]).then_inc(q_in[half], DMA)

        def branch(engine, ops, g, part):
            w = slice(2 * part, 2 * part + 2)
            if part == 0:
                engine.wait_ge(av_ok, HEADS * (g + 1))
            engine.wait_ge(m_read, 6 * g + part + 1)
            ops.tensor_tensor(av[:, w, :], av[:, w, :], rg[:, :, :], ALU.mult).then_inc(gated, 1)
            engine.wait_ge(a_hi_ok, 2 * g + part + 1)
            ops.tensor_tensor(a_lo[:, w, :], av[:, w, :], f32(a_hi[:, w, :]), ALU.subtract).then_inc(a_lo_ok, 1)

        @block.sync
        def _(sp):
            def load_k(g, slot):
                for part in range(2):
                    sp.dma_start(f32(ks[part * HEAD_DIM:(part + 1) * HEAD_DIM, :, 2 * slot:2 * slot + 2, :]).rearrange("p h a t -> p h (a t)"),
                                 D["k"][part].rearrange(rows, d=HEAD_DIM)[:, :, bass.ds(g * SUB + PAD, SUB)]).then_inc(k_in[slot % 2], DMA)

            def load_v(g, slot):
                sp.dma_start(f32(vs[:, 2 * slot:2 * slot + 2, :]),
                             D["v"][bass.ds(g * SUB, SUB), :].rearrange("(a p) c -> p a c", p=P)).then_inc(v_in[slot % 2], DMA)

            def load_ga(g):
                sp.dma_start(ga[:, :, :], D["ga"].rearrange("(c p) t -> p c t", p=P)[:, :, bass.ds(g * SUB + PAD, SUB)]).then_inc(ga_in, DMA)

            def load_yc(g):
                sp.dma_start(y[:, :, :], D["yc"][bass.ds(g * SUB, SUB), :].rearrange("(a p) d -> p a d", p=P)).then_inc(yc_in, DMA)

            def load_x(g):
                sp.dma_start(x[:, :, :], io["x"][0][bass.ds(g * SUB, SUB), :].rearrange("(a p) d -> p a d", p=P)).then_inc(x_in, DMA)

            def store(g):
                sp.wait_ge(sum_ok, 2 * (g + 1))
                sp.dma_start(out[0][bass.ds(g * SUB, SUB), :].rearrange("(a p) d -> p a d", p=P), x[:, :, :]).then_inc(x_out, DMA)

            load_k(0, 0)
            copies, entries = D["rev"].shape[1:]
            near = bass.AP(D["rev"].tensor, P - 1, [[entries - 1, P], [copies * entries, HEADS], [1, 2 * P]])
            sp.dma_start(bias[:, :, 3 * P:], near).then_inc(bias_in, DMA)
            sp.dma_start(far[:, :], io["rel_bias"][0][:, 2 * MAX_REL].partition_broadcast(P),
                         allow_slow_non_contiguous=True).then_inc(far_in, DMA)
            load_q(sp, 0, 1)
            load_v(0, 0)
            load_k(1, 1)
            load_ga(0)
            sp.dma_start(g_post[:, :], io["post_norm_g"][0].partition_broadcast(P)).then_inc(post_in, DMA)
            load_yc(0)
            W.load(sp)
            sp.wait_ge(W.w_lo, CT)
            load_x(0)

            def body(g, quad, slot):
                if not is_first(g):
                    sp.wait_ge(o_ps, HEADS * g)
                    if not is_last(g):
                        load_k(g + 1, (slot + 1) % 4)
                if not is_last(g):
                    load_v(g + 1, (slot + 1) % 4)
                if not is_first(g):
                    sp.wait_ge(m_read, 6 * (g - 1) + 2)
                    load_ga(g)
                if not is_last(g):
                    for half in range(2):
                        sp.wait_ge(s_ps, 16 * g + 8 * (half + 1))
                        load_q(sp, g + 1, half)
                if not is_first(g):
                    sp.wait_ge(sum_ok, 2 * g)
                    load_yc(g)
                    store(g - 1)
                    sp.wait_ge(x_out, DMA * g)
                    load_x(g)

            all_groups(sp, body)
            for t in range(2):
                sp.wait_ge(sum_ok, 2 * (NG - 1) + t + 1)
                sp.dma_start(out[0][(NG - 1) * SUB + t * P:(NG - 1) * SUB + (t + 1) * P, :], x[:, t, :]).then_inc(x_out, DMA)
            sp.wait_ge(x_out, DMA * (NG + 1))

        @block.gpsimd
        def _(pool):
            for j in range(2):
                for pt in (pt_hi, pt_lo):
                    for blind in (pt[j][:, 0, P:], pt[j][:, WT, 0:P]):
                        nc.gpsimd.tensor_tensor(blind, K["ident"][:, :], K["ident"][:, :], ALU.subtract).then_inc(zero_ok, 1)
            pool.wait_ge(zero_ok, 8)

            def last_rstd(t):
                pool.wait_ge(ss_ok, 4 * (NG - 1) + 2 * (t + 1))
                nc.gpsimd.tensor_tensor(ms[:, t:t + 1], ss[:, 2 * t:2 * t + 1], ss[:, 2 * t + 1:2 * t + 2], ALU.add).then_inc(ms_ok, 1)
                pool.wait_ge(ms_ok, 2 * (NG - 1) + 2 * t + 1)
                nc.gpsimd.tensor_tensor(mse[:, t:t + 1], ms[:, t:t + 1], K["eps"][:, 0:1], ALU.add).then_inc(ms_ok, 1)
                pool.wait_ge(ms_ok, 2 * (NG - 1) + 2 * t + 2)
                nc.gpsimd.tensor_tensor(rstd[:, t:t + 1], mse[:, t:t + 1], K["mhalf"][:, 0:1], ALU.pow).then_inc(rstd_ok, 1)

            def finish(g):
                pool.wait_ge(ss_ok, 4 * (g + 1))
                nc.gpsimd.tensor_tensor(ms[:, :], ss[:, 0:4:2], ss[:, 1:4:2], ALU.add).then_inc(ms_ok, 1)
                pool.wait_ge(ms_ok, 2 * g + 1)
                nc.gpsimd.tensor_tensor(mse[:, :], ms[:, :], K["eps"][:, 0:2], ALU.add).then_inc(ms_ok, 1)
                pool.wait_ge(ms_ok, 2 * g + 2)
                nc.gpsimd.tensor_tensor(rstd[:, :], mse[:, :], K["mhalf"][:, 0:2], ALU.pow).then_inc(rstd_ok, 1)
                gain(g, 0)
                add(g, 0)
                gain(g, 1)

            def gain(g, t):
                pool.wait_ge(yn_ok, 2 * g + t + 1)
                nc.gpsimd.tensor_tensor(y[:, t, :], y[:, t, :], g_post[:, :], ALU.mult).then_inc(yg_ok, 1)

            def add(g, t):
                pool.wait_ge(x_in, DMA * (g + 1))
                pool.wait_ge(yg_ok, 2 * g + t + 1)
                nc.gpsimd.tensor_tensor(x[:, t, :], x[:, t, :], y[:, t, :], ALU.add).then_inc(sum_ok, 1)

            def body(g):
                branch(pool, nc.gpsimd, g, 0)
                if not is_first(g):
                    add(g - 1, 1)
                branch(pool, nc.gpsimd, g, 1)
                finish(g)

            pool.wait_ge(post_in, DMA)
            body(0)
            with pool.Fori(1, NG - 1) as g:
                body(g)
            add(NG - 2, 1)
            for t in range(2):
                last_rstd(t)

        @block.scalar
        def _(act):
            def exp(g, slot, h, t):
                n, w = 16 * g + 2 * h + t, len(tiles_of(g, t)) * P
                act.wait_ge(max_ok, n + 1)
                nc.scalar.activation(pr[t][:, 0:w], pr[t][:, 0:w], ACT.Exp, bias=nmax[:, 2 * h + t:2 * h + t + 1], scale=-1.0,
                                     accum_out=psum_[slot % 2][:, t, h:h + 1]).then_inc(exp_ok, 1)

            def hi(g, h, t):
                n, js = 16 * g + 2 * h + t, tiles_of(g, t)
                act.wait_ge(t_ps, n + 1)
                if not (is_first(g) and h < 2):
                    act.wait_ge(o_ps, HEADS * g + h - 1)
                nc.scalar.activation(pt_hi[h % 2][:, js[0]:js[-1] + 1, t * P:(t + 1) * P],
                                     t_b[t][:, 0:len(js) * P].rearrange("p (j q) -> p j q", q=P), ACT.Copy).then_inc(hi_ok, 1)

            def lower(g, h):
                o = (h % 2) * HEAD_DIM
                act.wait_ge(o_ps, HEADS * g + h + 1)
                if not (is_first(g) and h < 2):
                    act.wait_ge(av_ok, HEADS * g + h - 1)
                nc.scalar.activation(low[o:o + HEAD_DIM, :], o_bank(h)[HEAD_DIM:, :], ACT.Copy).then_inc(low_ok, 1)

            def tail(g, part, t=None):
                if part in (0, 1):
                    act.wait_ge(gated, 2 * g + part + 1)
                    nc.scalar.activation(a_hi[:, 2 * part:2 * part + 2, :], av[:, 2 * part:2 * part + 2, :], ACT.Copy).then_inc(a_hi_ok, 1)
                elif part == "norm":
                    act.wait_ge(rstd_ok, g + 1)
                    nc.scalar.activation(y[:, t, :], y[:, t, :], ACT.Copy, scale=rstd[:, t:t + 1]).then_inc(yn_ok, 1)
                else:
                    u = part - 2
                    act.wait_ge(m_read, 6 * g + 2 + u + 1)
                    if not (is_first(g) and u == 0):
                        act.wait_ge(ss_ok, 4 * g + u)
                    nc.scalar.activation(junk[:, :], y[:, u // 2, (u % 2) * D_HALF:(u % 2 + 1) * D_HALF], ACT.Square,
                                         scale=D_MODEL ** -0.5, accum_out=ss[:, u:u + 1]).then_inc(ss_ok, 1)

            load_q(act, 0, 0)
            exp(0, 0, 0, 0)
            exp(0, 0, 0, 1)

            def body(g, quad, slot):
                for h in range(HEADS):
                    for t in range(2):
                        hi(g, h, t)
                        if t == 1 and not (is_first(g) and h == 0):
                            lower(g - (h == 0), (h - 1) % HEADS)
                        if h < HEADS - 1:
                            exp(g, slot, h + 1, t)
                        elif not is_last(g):
                            exp(g + 1, (slot + 1) % 4, 0, t)
                        if not is_first(g):
                            if (h, t) in ((1, 0), (2, 0)):
                                tail(g - 1, h - 1)
                            if y_slot(h, t) is not None:
                                for u in Y_DONE[y_slot(h, t)]:
                                    tail(g - 1, 2 + u)
                            if h == HEADS - 1:
                                tail(g - 1, "norm", t)
                    if is_first(g):
                        if h < CT:
                            W.split_hi(act, h, h + 1)

            all_groups(act, body)
            lower(NG - 1, HEADS - 1)
            for part in range(6):
                tail(NG - 1, part)

        @block.vector
        def _(dve):
            dve.wait_ge(bias_in, DMA)
            dve.wait_ge(far_in, DMA)
            nc.vector.tensor_copy(bias[:, :, 0:3 * P], far[:, :, None].broadcast_to([P, HEADS, 3 * P])).then_inc(bias_ok, 1)
            dve.wait_ge(bias_ok, 1)
            nc.vector.memset(bias[CHUNK:, :, 0:CHUNK], MASKED).then_inc(bias_ok, 1)
            nc.vector.memset(bias[0:CHUNK, :, WT * P - CHUNK:], MASKED).then_inc(bias_ok, 1)
            dve.wait_ge(bias_ok, 3)

            def maximum(g, slot, h, t):
                n, js = 16 * g + 2 * h + t, tiles_of(g, t)
                w, (both, n0) = len(js) * P, pieces(slot, js)
                o = 0 if len(both) == 1 else 512 - n0 * P
                dve.wait_ge(s_ps, n + 1)
                if not (is_first(g) and h == 0):
                    dve.wait_ge(t_ps, n - 1)
                dve.sem_inc(max_begun, 1)
                nc.vector.tensor_tensor_reduce(out=pr[t][:, 0:w], in0=s_b[:, o:o + w], in1=bias[:, h, WT * P - w:],
                                               scale=-1.0, scalar=3e38, op0=ALU.add, op1=ALU.min,
                                               accum_out=nmax[:, 2 * h + t:2 * h + t + 1]).then_inc(max_ok, 1)

            def lo(g, h, t):
                n, js = 16 * g + 2 * h + t, tiles_of(g, t)
                dst = slice(js[0], js[-1] + 1), slice(t * P, (t + 1) * P)
                dve.wait_ge(hi_ok, n + 1)
                nc.vector.tensor_tensor(pt_lo[h % 2][:, dst[0], dst[1]], t_b[t][:, 0:len(js) * P].rearrange("p (j q) -> p j q", q=P),
                                        f32(pt_hi[h % 2][:, dst[0], dst[1]]), ALU.subtract).then_inc(lo_ok, 1)

            def merge(g, h):
                o = (h % 2) * HEAD_DIM
                dve.wait_ge(low_ok, HEADS * g + h + 1)
                if h % 4 == 0 and not is_first(g):
                    dve.wait_ge(a_lo_ok, 2 * g - 1 + h // 4)
                nc.vector.tensor_tensor(av[o:o + HEAD_DIM, h // 2, :], o_bank(h)[0:HEAD_DIM, :], low[o:o + HEAD_DIM, :],
                                        ALU.add).then_inc(av_ok, 1)

            def tail(g, slot, part):
                if part == "rec":
                    dve.wait_ge(exp_ok, 16 * (g + 1))
                    nc.vector.reciprocal(rec[:, :, :], psum_[slot % 2][:, :, :]).then_inc(rec_ok, 1)
                    dve.wait_ge(rec_ok, g + 1)
                    for half in range(2):
                        hs = slice(4 * half, 4 * half + 4)
                        nc.vector.tensor_scalar(recx[:, 2 * half:2 * half + 2, :].rearrange("p t (h d) -> p t h d", d=HEAD_DIM),
                                                rec[:, :, hs, None].broadcast_to([P, 2, 4, HEAD_DIM]), 0.5, None, ALU.mult).then_inc(recx_ok, 1)
                elif part in (0, 1):
                    w = slice(2 * part, 2 * part + 2)
                    dve.wait_ge(r_ps, 2 * g + part + 1)
                    if part == 0:
                        dve.wait_ge(ga_in, DMA * (g + 1))
                    if part > 0 or not is_first(g):
                        dve.wait_ge(gated, 2 * g + part)
                    nc.vector.tensor_tensor(rg[:, :, :], m_b[:, :].rearrange("p (c t) -> p c t", c=2), ga[:, w, :], ALU.mult).then_inc(m_read, 1)
                else:
                    u = part - 2
                    yv = y[:, u // 2, (u % 2) * D_HALF:(u % 2 + 1) * D_HALF]
                    dve.wait_ge(y_ps, 4 * g + u + 1)
                    if u == 0:
                        dve.wait_ge(yc_in, DMA * (g + 1))
                    nc.vector.tensor_tensor(yv, y_bank(g, u), yv, ALU.add).then_inc(m_read, 1)

            def last_finish(t):
                if t == 0:
                    dve.wait_ge(post_in, DMA)
                    dve.wait_ge(x_in, DMA * NG)
                dve.wait_ge(rstd_ok, NG + t)
                nc.vector.scalar_tensor_tensor(y[:, t, :], y[:, t, :], rstd[:, t:t + 1], g_post[:, :], ALU.mult, ALU.mult).then_inc(yn_ok, 1)
                dve.wait_ge(yn_ok, 2 * (NG - 1) + t + 1)
                nc.vector.tensor_tensor(x[:, t, :], x[:, t, :], y[:, t, :], ALU.add).then_inc(sum_ok, 1)

            maximum(0, 0, 0, 0)
            maximum(0, 0, 0, 1)

            def body(g, quad, slot):
                for h in range(HEADS):
                    if h == 0 and not is_first(g):
                        tail(g - 1, slot - 1, "rec")
                    for t in range(2):
                        if y_slot(h, t) is not None and not is_first(g):
                            for u in Y_DONE[y_slot(h, t)]:
                                tail(g - 1, slot - 1, 2 + u)
                        if h < HEADS - 1:
                            maximum(g, slot, h + 1, t)
                        elif not is_last(g):
                            maximum(g + 1, (slot + 1) % 4, 0, t)
                        lo(g, h, t)
                    if not (is_first(g) and h == 0):
                        merge(g - (h == 0), (h - 1) % HEADS)
                    if is_first(g):
                        if h < CT:
                            W.split_lo(dve, h, h + 1)
                    elif h < 2:
                        tail(g - 1, slot - 1, h)

            all_groups(dve, body)
            merge(NG - 1, HEADS - 1)
            for part in ("rec", 0, 1, 2, 3, 4):
                tail(NG - 1, (NG - 1) % 4, part)
                if part in (0, 1):
                    branch(dve, nc.vector, NG - 1, part)
            last_finish(0)
            tail(NG - 1, (NG - 1) % 4, 5)
            last_finish(1)

        @block.tensor
        def _(pe):
            def scores(g, quad, slot, h, t):
                n, js = 16 * g + 2 * h + t, tiles_of(g, t)
                both, n0 = pieces(slot, js)
                if h % 4 == 0 and t == 0:
                    pe.wait_ge(q_in[h // 4], 4 * DMA * (g + 1))
                if h == 0 and t == 0:
                    pe.wait_ge(k_in[slot % 2], 2 * DMA * (2 * quad + slot // 2 + 1))
                if not (is_first(g) and h == 0 and t == 0):
                    pe.wait_ge(max_ok, n)
                o = 0 if len(both) == 1 else 512 - n0 * P
                for piece, count in zip(both, (n0, len(js) - n0)):
                    for part in (q_hi, q_lo):
                        mm = nc.tensor.matmul(s_b[:, o:o + count * P], part[:, h, t * P:(t + 1) * P], ks[:, h, piece, :],
                                              start=(part is q_hi), stop=(part is q_lo))
                    o += count * P
                mm.then_inc(s_ps, 1)

            def turn(g, h, t):
                n, js = 16 * g + 2 * h + t, tiles_of(g, t)
                pe.wait_ge(exp_ok, n + 1)
                if not (is_first(g) and h == 0):
                    pe.wait_ge(lo_ok, n - 1)
                for j in range(len(js)):
                    mm = nc.tensor.transpose(t_b[t][:, j * P:(j + 1) * P], pr[t][:, j * P:(j + 1) * P], K["ident"][:, :])
                mm.then_inc(t_ps, 1)

            def weigh(g, quad, slot, h, half):
                js = [j for j in range(WT + 1) if j in tiles_of(g, 0) + tiles_of(g, 1)]
                if half == 0:
                    pe.wait_ge(lo_ok, 16 * g + 2 * h + 2)
                    if h == 0:
                        pe.wait_ge(v_in[slot % 2], DMA * (2 * quad + slot // 2 + 1))
                        if is_first(g):
                            pe.wait_ge(zero_ok, 8)
                    if h == HEADS - 2:
                        if not is_first(g):
                            pe.wait_ge(m_read, 6 * g)
                    elif not (is_first(g) and h == 0):
                        pe.wait_ge(av_ok, HEADS * g + (h if h < HEADS - 1 else h - 1))
                for j in js[:len(js) // 2] if half == 0 else js[len(js) // 2:]:
                    for part in (pt_hi, pt_lo):
                        mm = nc.tensor.matmul(o_bank(h), vs[:, ring(slot, j), h * P:(h + 1) * P], part[h % 2][:, j, :],
                                              start=(j == js[0] and part is pt_hi), stop=(j == js[-1] and part is pt_lo))
                if half == 1:
                    mm.then_inc(o_ps, 1)

            def spread(g, part):
                pe.wait_ge(recx_ok, 2 * g + part + 1)
                if part == 0:
                    pe.wait_ge(av_ok, HEADS * g + HEADS - 1)
                else:
                    pe.wait_ge(m_read, 6 * g + part)
                for pair in range(2):
                    for t in range(2):
                        mm = nc.tensor.matmul(m_b[:, pair * SUB + t * P:pair * SUB + (t + 1) * P],
                                              recx[:, 2 * part + t, pair * P:(pair + 1) * P], K["ident"][:, :],
                                              start=True, stop=True)
                mm.then_inc(r_ps, 1)

            def project(g, steps):
                for u, k in (divmod(s, CT) for s in steps):
                    if u == 0 and k % 2 == 0:
                        pe.wait_ge(a_lo_ok, 2 * g + k // 2 + 1)
                    if u == 0 and k == 0 and is_first(g):
                        pe.wait_ge(W.w_lo, CT)
                    if k == 0 and not (is_last(g) and u > 0):
                        pe.wait_ge(m_read, 6 * g + 2 + u)
                    w, n = slice((u // 2) * P, (u // 2 + 1) * P), slice((u % 2) * D_HALF, (u % 2 + 1) * D_HALF)
                    nc.tensor.matmul(y_bank(g, u), a_hi[:, k, w], wo_hi[:, k, n], start=(k == 0), stop=False)
                    nc.tensor.matmul(y_bank(g, u), a_hi[:, k, w], wo_lo[:, k, n], start=False, stop=False)
                    mm = nc.tensor.matmul(y_bank(g, u), a_lo[:, k, w], wo_hi[:, k, n], start=False, stop=(k == CT - 1))
                    if k == CT - 1:
                        mm.then_inc(y_ps, 1)

            scores(0, 0, 0, 0, 0)
            scores(0, 0, 0, 0, 1)

            def body(g, quad, slot):
                nxt = (g + 1, quad + (slot == 3), (slot + 1) % 4)
                for h in range(HEADS):
                    for t in range(2):
                        turn(g, h, t)
                        if h < HEADS - 1:
                            scores(g, quad, slot, h + 1, t)
                        elif not is_last(g):
                            scores(*nxt, 0, t)
                        if h > 0:
                            weigh(g, quad, slot, h - 1, t)
                        elif not is_first(g):
                            weigh(g - 1, quad - (slot == 0), (slot - 1) % 4, HEADS - 1, t)
                        if not is_first(g):
                            if h < 2 and t == 0:
                                spread(g - 1, h)
                            if y_slot(h, t) in range(n_slots):
                                project(g - 1, Y_STEPS[y_slot(h, t)])

            all_groups(pe, body)
            for half in range(2):
                weigh(NG - 1, (NG - 1) // 4, (NG - 1) % 4, HEADS - 1, half)
            for part in range(2):
                spread(NG - 1, part)
            project(NG - 1, range(4 * CT))


def build(nc, io, out):
    def scratch(name, shape, dt=F32):
        return nc.dram_tensor(name, shape, dt, kind="Internal").ap()

    D = {
        "q": scratch("q_parts", [2, D_HALF, PAD + SEQ]),
        "k": scratch("k_parts", [2, D_HALF, PAD + SEQ]),
        "v": scratch("v_parts", [SEQ, 2 * D_HALF]),
        "hg": scratch("glu", [D_HALF, PAD + SEQ]),
        "acc": scratch("conv_part", [D_HALF, PAD + SEQ]),
        "acc2": scratch("conv", [D_HALF, PAD + SEQ]),
        "ga": scratch("gate_att", [D_HALF, PAD + SEQ]),
        "gc": scratch("gate_conv", [D_HALF, PAD + SEQ]),
        "rev": scratch("rel_bias_reversed", [HEADS, P, 3 * P - 1]),
        "yc": scratch("y_conv", [SEQ, D_MODEL]),
    }
    with ExitStack() as ctx:
        T = Tools(nc, ctx, "k")
        K = {name: T.sb(name, [P, cols]) for name, cols in (
            ("ident", P), ("ones", P), ("eps", 4), ("mhalf", 4), ("g_pre", KT), ("dw_b", CT), ("ln_g", CT), ("ln_b", CT),
            ("b_pw", CT), ("ln_gh", CT), ("ln_bh", CT), ("b_pw2", CT), ("dwt", CT * TAPS))}
        setup(nc, io, K, D)
        with ExitStack() as shared:
            H = Hidden(nc, Tools(nc, shared, "h"), K, io["x"][0])
            pass_1(nc, io, K, D, H)
            pass_2(nc, io, K, D, H)
        pass_3(nc, io, K, D)
        pass_4(nc, io, K, D, out)


NAMES = ["x", "pre_norm_g", "w_in", "rel_bias", "dw_w", "dw_b", "conv_ln_g", "conv_ln_b", "w_pw", "b_pw", "w_out",
         "post_norm_g"]


def kernel(**inputs):
    import numpy as np
    import concourse.bacc as bacc
    from concourse.bass_utils import run_bass_kernel_spmd

    nc = bacc.Bacc("TRN2", target_bir_lowering=False, num_devices=1)
    arrays, io = {}, {}
    for name in NAMES:
        a = np.ascontiguousarray(inputs[name])
        arrays[f"in_{name}"] = a
        io[name] = nc.dram_tensor(f"in_{name}", a.shape, mybir.dt.from_np(a.dtype), kind="ExternalInput").ap()
    out = nc.dram_tensor("out", inputs["x"].shape, F32, kind="ExternalOutput").ap()
    build(nc, io, out)
    r = run_bass_kernel_spmd(nc, [arrays], core_ids=[0])
    return r.results[0]["out"]
```
